# Optimizing a Trainium2 kernel written in Bass

```python
import jax, jax.numpy as jnp
from jax import lax
import numpy as np

D_MODEL = 2048
BATCH = 1
SEQ = 256
DEPTH = 1

N_META = 16
D_ATTN = D_MODEL // 2
N_HEADS_SB = 16
HEAD_DIM_SB = D_ATTN // N_HEADS_SB
D_POOL = D_MODEL // 4
POOL_WINDOWS = (2, 4, 8, 16)
N_POOL_GROUPS = len(POOL_WINDOWS)
POOL_GROUP_DIM = D_POOL // N_POOL_GROUPS
D_CONV = D_MODEL // 4
CONV_WIDTH = 31
D_MIX = D_ATTN + D_POOL + D_CONV
D_IN_PROJ = 3 * D_ATTN + D_POOL + 2 * D_CONV
D_FF = ((8 * D_MODEL + 3 * 256 - 1) // (3 * 256)) * 256
BLOCK_Q = 128
EPS = 1e-6

kernel_name = "hybrid_stickbreak_pool_conformer_trunk"

def rmsnorm(x, g):
    xf = x.astype(jnp.float32)
    y = xf * lax.rsqrt(jnp.mean(xf * xf, axis=-1, keepdims=True) + EPS)
    return (y * g.astype(jnp.float32)).astype(x.dtype)

def layernorm(x, g, b):
    xf = x.astype(jnp.float32)
    mu = jnp.mean(xf, axis=-1, keepdims=True)
    var = jnp.mean(jnp.square(xf - mu), axis=-1, keepdims=True)
    y = (xf - mu) * lax.rsqrt(var + EPS)
    return (y * g.astype(jnp.float32) + b.astype(jnp.float32)).astype(x.dtype)

def stick_breaking_attention(q, k, v):
    b, l, h, dh = q.shape
    pad = (-l) % BLOCK_Q
    padw = ((0, 0), (pad, 0), (0, 0), (0, 0))
    qf = jnp.pad(q.astype(jnp.float32) * (dh ** -0.5), padw)
    kf = jnp.pad(k.astype(jnp.float32), padw)
    vf = jnp.pad(v.astype(jnp.float32), padw)
    lp = l + pad
    n_blocks = lp // BLOCK_Q
    key_pos = jnp.arange(lp) - pad

    def one_block(i):
        q_blk = lax.dynamic_slice_in_dim(qf, i * BLOCK_Q, BLOCK_Q, axis=1)
        q_pos = i * BLOCK_Q + jnp.arange(BLOCK_Q) - pad
        z = jnp.einsum('bqhd,bkhd->bhqk', q_blk, kf)
        mask = (key_pos[None, :] < q_pos[:, None]) & (key_pos[None, :] >= 0)
        log_not_beta = jnp.where(mask, -jax.nn.softplus(z), 0.0)
        later = lax.cumsum(log_not_beta, axis=3, reverse=True) - log_not_beta
        weights = jnp.where(mask, jnp.exp(jax.nn.log_sigmoid(z) + later), 0.0)
        return jnp.einsum('bhqk,bkhd->bqhd', weights, vf)

    out = lax.map(one_block, jnp.arange(n_blocks))
    out = jnp.moveaxis(out, 0, 1).reshape(b, lp, h, dh)[:, pad:]
    return out.astype(v.dtype)

def multiscale_pool(u, w_pool, pool_scale):
    b, l, _ = u.shape
    uf = u.astype(jnp.float32)
    cs = jnp.pad(jnp.cumsum(uf, axis=1), ((0, 0), (1, 0), (0, 0)))
    t = jnp.arange(l)
    groups = []
    for g, w in enumerate(POOL_WINDOWS):
        lo, hi = g * POOL_GROUP_DIM, (g + 1) * POOL_GROUP_DIM
        start = jnp.maximum(t + 1 - w, 0)
        csg = cs[:, :, lo:hi]
        window_sum = csg[:, 1:] - csg[:, start]
        count = (t + 1 - start).astype(jnp.float32)[None, :, None]
        groups.append(window_sum / count - uf[:, :, lo:hi])
    pooled = jnp.stack(groups, axis=2)
    mixed = jnp.einsum('blgc,gcd->blgd', pooled, w_pool.astype(jnp.float32))
    mixed = mixed.reshape(b, l, D_POOL) * pool_scale.astype(jnp.float32)
    return mixed.astype(u.dtype)

def conformer_conv(u_glu, w_dw, b_dw, ln_g, ln_b, w_pw):
    a, gate = jnp.split(u_glu, 2, axis=-1)
    u = a * jax.nn.sigmoid(gate)
    y = lax.conv_general_dilated(
        u, w_dw[:, None, :].astype(u.dtype), window_strides=(1,),
        padding=[(CONV_WIDTH - 1, 0)],
        dimension_numbers=('NWC', 'WIO', 'NWC'),
        feature_group_count=D_CONV) + b_dw
    y = layernorm(y, ln_g, ln_b)
    y = jax.nn.silu(y)
    return y @ w_pw

def setup_inputs(seed: int = 0) -> dict:
    key = jax.random.key(seed)
    ks = jax.random.split(key, 20)
    f32 = jnp.float32

    def nrm(k, shape, scale):
        return jax.random.normal(k, shape, f32) * scale

    def gain(k, shape):
        return 1.0 + 0.05 * jax.random.normal(k, shape, f32)

    return {
        "x": nrm(ks[0], (BATCH, SEQ, D_MODEL), 1.0),
        "meta_tokens": nrm(ks[1], (N_META, D_MODEL), 1.0),
        "pre_mix_g": gain(ks[2], (DEPTH, D_MODEL)),
        "w_in": nrm(ks[3], (DEPTH, D_MODEL, D_IN_PROJ), D_MODEL ** -0.5),
        "w_pool": nrm(ks[4], (DEPTH, N_POOL_GROUPS, POOL_GROUP_DIM, POOL_GROUP_DIM), POOL_GROUP_DIM ** -0.5),
        "pool_scale": gain(ks[5], (DEPTH, D_POOL)),
        "w_dw": nrm(ks[6], (DEPTH, CONV_WIDTH, D_CONV), CONV_WIDTH ** -0.5),
        "b_dw": nrm(ks[7], (DEPTH, D_CONV), 0.02),
        "conv_ln_g": gain(ks[8], (DEPTH, D_CONV)),
        "conv_ln_b": nrm(ks[9], (DEPTH, D_CONV), 0.02),
        "w_pw": nrm(ks[10], (DEPTH, D_CONV, D_CONV), D_CONV ** -0.5),
        "mix_out_g": gain(ks[11], (DEPTH, D_MIX)),
        "w_out": nrm(ks[12], (DEPTH, D_MIX, D_MODEL), D_MIX ** -0.5),
        "post_mix_g": gain(ks[13], (DEPTH, D_MODEL)),
        "pre_ffn_g": gain(ks[14], (DEPTH, D_MODEL)),
        "w_gate": nrm(ks[15], (DEPTH, D_MODEL, D_FF), D_MODEL ** -0.5),
        "w_up": nrm(ks[16], (DEPTH, D_MODEL, D_FF), D_MODEL ** -0.5),
        "w_down": nrm(ks[17], (DEPTH, D_FF, D_MODEL), D_FF ** -0.5),
        "post_ffn_g": gain(ks[18], (DEPTH, D_MODEL)),
    }

def reference(x, meta_tokens, pre_mix_g, w_in, w_pool, pool_scale, w_dw, b_dw,
              conv_ln_g, conv_ln_b, w_pw, mix_out_g, w_out, post_mix_g,
              pre_ffn_g, w_gate, w_up, w_down, post_ffn_g):
    b = x.shape[0]
    meta = jnp.broadcast_to(meta_tokens[None].astype(x.dtype), (b, N_META, D_MODEL))
    h = jnp.concatenate([meta, x], axis=1)
    l = h.shape[1]
    splits = [D_ATTN, 2 * D_ATTN, 3 * D_ATTN, 3 * D_ATTN + D_POOL]

    for i in range(DEPTH):
        u = rmsnorm(h, pre_mix_g[i])
        proj = u @ w_in[i]
        q, k, v, u_pool, u_conv = jnp.split(proj, splits, axis=-1)
        heads = (b, l, N_HEADS_SB, HEAD_DIM_SB)
        o_attn = stick_breaking_attention(q.reshape(heads), k.reshape(heads), v.reshape(heads))
        o_attn = o_attn.reshape(b, l, D_ATTN)
        o_pool = multiscale_pool(u_pool, w_pool[i], pool_scale[i])
        o_conv = conformer_conv(u_conv, w_dw[i], b_dw[i], conv_ln_g[i], conv_ln_b[i], w_pw[i])
        g = mix_out_g[i]
        merged = jnp.concatenate([
            rmsnorm(o_attn, g[:D_ATTN]),
            rmsnorm(o_pool, g[D_ATTN:D_ATTN + D_POOL]),
            rmsnorm(o_conv, g[D_ATTN + D_POOL:]),
        ], axis=-1)
        h = h + rmsnorm(merged @ w_out[i], post_mix_g[i])

        u = rmsnorm(h, pre_ffn_g[i])
        ff = (jax.nn.silu(u @ w_gate[i]) * (u @ w_up[i])) @ w_down[i]
        h = h + rmsnorm(ff, post_ffn_g[i])

    return h[:, N_META:]


_drawn_inputs = setup_inputs


def setup_inputs(seed=0):
    import zlib

    import numpy as np

    out = dict(_drawn_inputs(seed))
    spreads = {}
    factors = {'pool_scale': 2.684, 'b_dw': 3.513, 'conv_ln_b': 7.02}
    for name, (base, spread) in spreads.items():
        noise = np.random.default_rng([zlib.crc32(name.encode()), seed]).standard_normal(out[name].shape)
        drawn = base * np.exp(spread * noise) if base else spread * noise
        out[name] = __import__('jax').numpy.asarray(drawn.astype(out[name].dtype))
    for name, factor in factors.items():
        out[name] = (out[name] * factor).astype(out[name].dtype)
    return out
```

```python
from contextlib import ExitStack

import concourse.bass as bass
from concourse import mybir

F32 = mybir.dt.float32
F32R = mybir.dt.float32r
ALU = mybir.AluOpType
ACT = mybir.ActivationFunctionType
AX = mybir.AxisListType

P = 128
EPS = 1e-6
NEG = -1e30
WSLOTS = 4
CK = 4
BLK = 256
DCOLS = 512
LAG = 3


def build_trunk(nc, x, meta, pre_mix_g, w_in, w_pool, pool_scale, w_dw, b_dw, conv_ln_g, conv_ln_b, w_pw,
                mix_out_g, w_out, post_mix_g, pre_ffn_g, w_gate, w_up, w_down, post_ffn_g, out):
    _, SEQ, D = x.shape
    META = meta.shape[0]
    TOK = META + SEQ
    NQ = SEQ // P
    KT = D // P
    TAPS, DC = w_dw.shape[1], w_dw.shape[2]
    NPG, PG = w_pool.shape[1], w_pool.shape[2]
    DP = NPG * PG
    DA = D - DP - DC
    DH = 64
    FF = w_gate.shape[2]
    FT = FF // P
    CT = DC // P
    PT = DP // P
    KPAD = 3 * P
    GROUPS = DA // BLK
    HPG = BLK // DH
    assert NQ == 2 and P < TOK - P and TOK <= KPAD and PG == P

    Q_CONV = 0
    Q_POOL = Q_CONV + 4 * CK
    Q_ATT = Q_POOL + 2 * CK
    PER_G = 3 * CK
    Q_OUT = Q_ATT + GROUPS * PER_G
    FIRST = 5
    NOB = D // BLK
    Q_FFN = Q_OUT + NOB * CK
    NFB = FF // BLK
    Q_DOWN = Q_FFN + 2 * CK * NFB
    DN = D // DCOLS
    DCH = FT // 2
    SC = (Q_ATT + PER_G)
    C_POOL, C_A, C_GATE = 3 * DA, 3 * DA + DP, 3 * DA + DP + DC

    def attn_at(n):
        g, h = n // HPG, n % HPG
        if g == GROUPS - 1:
            return Q_OUT + 1 + h + h // 2
        return SC + PER_G * g + 1 + 2 * h
    NH = GROUPS * HPG
    HEAD_AT = {attn_at(n): n for n in range(NH)}
    VT_AT = {SC + PER_G * g - 1: g for g in range(GROUPS)}
    Q_TAPS = Q_POOL + CK
    PE_MIX = Q_POOL + 14
    PE_SSP = Q_POOL + 18
    PE_LNM = Q_TAPS + TAPS - 1
    PE_LNV = PE_LNM + 4
    PE_PW = PE_LNV + 9
    PE_SSC = PE_PW + 6
    PE_SSA = Q_OUT + 12

    out_parts = [("side", j) for j in range(FIRST)] + [("attn", j) for j in range(FIRST)] + \
                [("side", j) for j in range(FIRST, NOB)] + [("attn", j) for j in range(FIRST, NOB)]
    OC = CK // 2
    turn_bank = (4, 5, 7)
    side_bank = [0, 1, 2, 3, 4, 2, 3, 4]
    attn_bank = [5, 6, 7, 0, 1, 5, 6, 7]
    OUT_EVAC = {Q_OUT + OC * n + OC - 1 + 4: j for n, (part, j) in enumerate(out_parts) if part == "attn"}

    with ExitStack() as ctx:
        top = [(nc.sbuf_base + 63) // 64 * 64]

        def place(nbytes):
            at = top[0]
            top[0] += nbytes
            return at

        def sb_at(name, shape, dt, at):
            return nc.alloc_sbuf_tensor_at(name, shape, dt, offset=at)

        CE = CK * BLK
        raw = sb_at("raw", [P, WSLOTS, CE], F32, place(4 * WSLOTS * CE))
        w_hi = sb_at("w_hi", [P, WSLOTS, CE], F32R, place(4 * WSLOTS * CE))
        w_lo = sb_at("w_lo", [P, WSLOTS, CE], F32R, place(4 * WSLOTS * CE))
        a_in = place(4 * KT * 2 * TOK)
        u = sb_at("u", [P, KT, 2, TOK], F32R, a_in)
        f_acc = sb_at("f_acc", [P, NQ, D], F32, a_in)
        a_xt = place(4 * KT * SEQ)
        xT = sb_at("xT", [P, KT, SEQ], F32, a_xt)
        gbc = sb_at("gbc", [P, D], F32, a_xt)
        tmp_ffn = sb_at("tmp_ffn", [P, 4, 2 * SEQ], F32, a_xt + 4 * D)
        a_y = place(4 * KT * SEQ)
        y = sb_at("y", [P, KT, SEQ], F32, a_y)
        h2rows = sb_at("h2rows", [P, NQ, D], F32, a_y)
        side = sb_at("side", [P, KT * SEQ], F32, a_y)
        a_c = place(4 * 1152)
        cst = sb_at("cst", [P, 1152], F32, a_c)
        a_ff = place(4 * FT * 2 * SEQ)
        ffn = sb_at("ffn", [P, FT, 2, SEQ], F32R, a_ff)
        AR = (FT - KT) * 2 * SEQ
        arena = sb_at("arena", [P, AR], F32, a_ff + 4 * KT * 2 * SEQ)
        assert top[0] <= nc.sbuf_usable_end

        def carve(tensor, at, *dims):
            n = 1
            for d in dims:
                n *= d
            ap = tensor[:, at:at + n]
            if len(dims) == 2:
                ap = ap.rearrange("p (a b) -> p a b", a=dims[0])
            if len(dims) == 3:
                ap = ap.rearrange("p (a b c) -> p a b c", a=dims[0], b=dims[1])
            return ap, at + n

        ident, c = carve(cst, 0, P)
        ones, c = carve(cst, c, P)
        NV = 4 * KT + PT + 3 * CT
        vec, c = carve(cst, c, NV)
        dw, c = carve(cst, c, TAPS * CT)
        eps, c = carve(cst, c, 1)
        ss0, c = carve(cst, c, 3)
        r0, c = carve(cst, c, 3)
        ssd, c = carve(cst, c, NQ, DN)
        sst, c = carve(cst, c, NQ)
        rd, c = carve(cst, c, NQ)
        dummy, c = carve(cst, c, 1)
        r2, c = carve(cst, c, 2, SEQ)
        assert c <= 1152
        V_PRE, V_MIX, V_POST, V_FFN = 0, KT, 2 * KT, 3 * KT
        V_PS, V_BDW = 4 * KT, 4 * KT + PT
        V_LNG, V_LNB = V_BDW + CT, V_BDW + 2 * CT
        wpw, c = carve(side, 0, CT, DC)
        wpl, c = carve(side, c, NPG, PG)
        sq4, c = carve(side, c, CT, SEQ)
        acc_o, c = carve(side, c, SEQ)
        sq_o, c = carve(side, c, SEQ)
        assert c <= KT * SEQ
        GP = TAPS - 1
        SM = TOK - META + (TOK - P) + (TOK - 2 * P)
        S0, S1, S2 = 0, TOK - META, TOK - META + TOK - P
        glu, c = carve(arena, 0, CT, GP + TOK)
        junk = arena[:, c:c + D]
        cy, c = carve(arena, c, CT, SEQ)
        mf, c = carve(arena, c, CT, SEQ)
        mask, c = carve(arena, c, SM)
        negtri, c = carve(arena, c, P)
        negones, c = carve(arena, c, P)
        rside, c = carve(arena, c, SEQ)
        ra, c = carve(arena, c, 2, SEQ)
        qb, kb, vb, vT = [None] * 2, [None] * 2, [None] * 2, [None] * 2
        u_f, _ = carve(arena, c, 4, TOK)
        r0b, _ = carve(arena, c + 4 * TOK, TOK)
        vrow, _ = carve(arena, c + 5 * TOK, P)
        drow, _ = carve(arena, c + 5 * TOK + P, P)
        diag, _ = carve(arena, c + 5 * TOK + 2 * P, 3, P)
        qb[0], c = carve(arena, c, 2, SEQ)
        kb[0], c = carve(arena, c, 2, KPAD)
        vb[0], c = carve(arena, c, 2, KPAD)
        vT[0], c = carve(arena, c, 3, BLK)
        over = c
        qb[1], c = carve(arena, c, 2, SEQ)
        kb[1], c = carve(arena, c, 2, KPAD)
        vb[1], c = carve(arena, c, 2, KPAD)
        vT[1], c = carve(arena, c, 3, BLK)
        zm, c = carve(arena, c, 2, SM)
        lg, c = carve(arena, c, SM)
        sp, c = carve(arena, c, 2, SM)
        lw, c = carve(arena, c, 2, SM)
        wt, c = carve(arena, c, 2, SM)
        assert c <= AR
        xr, e = carve(arena, over, 3, D)
        assert e <= c
        a_s, e = carve(arena, over, 2, TOK)
        sg, e = carve(arena, e, 2, TOK)
        pu, e = carve(arena, e, PT, TOK)
        pw0, e = carve(arena, e, PT, TOK)
        pw1, e = carve(arena, e, PT, TOK)
        pooled, e = carve(arena, e, PT, SEQ)
        assert e <= c
        tb, e = carve(arena, over, 2, SEQ)
        sqy, e = carve(arena, e, 2, SEQ)
        accy, e = carve(arena, e, 2, SEQ)
        r1, e = carve(arena, e, 2, SEQ)
        th, e = carve(arena, e, 2, 2, SEQ)
        assert e <= AR
        sqh, e = carve(arena, 0, KT // 2, 2 * SEQ)
        assert e <= over

        ps = ctx.enter_context(nc.psum_tensor("ps", [P, 8, 512], F32))

        def sem(name):
            return ctx.enter_context(nc.semaphore(name))

        slot_free = sem("slot_free")
        raw_landed = [sem(f"raw_landed{s}") for s in range(WSLOTS)]
        hi_done, lo_done, chunks_used = sem("hi_done"), sem("lo_done"), sem("chunks_used")
        x_landed, vec_landed, sw_landed, gbc_landed, stored = (
            sem("x_landed"), sem("vec_landed"), sem("sw_landed"), sem("gbc_landed"), sem("stored"))
        const_step, const_ready, pads_ready, pads0, lg_done = (
            sem("const_step"), sem("const_ready"), sem("pads_ready"), sem("pads0"), sem("lg_done"))
        ss0_done, r0_done, diag_done, r0b_made, r0b_done = (
            sem("ss0_done"), sem("r0_done"), sem("diag_done"), sem("r0b_made"), sem("r0b_done"))
        vec_turned, vec_done, xt_made, xt_kept, uf_done, u_hi, u_lo = (
            sem("vec_turned"), sem("vec_done"), sem("xt_made"), sem("xt_kept"), sem("uf_done"), sem("u_hi"), sem("u_lo"))
        a_kept, gate_sig, glu_done, tap_done = sem("a_kept"), sem("gate_sig"), sem("glu_done"), sem("tap_done")
        pu_kept, pool_step, mix_made, pm_done, ssp_made, rp_done, pn_done, pool_hi, pool_lo = (
            sem("pu_kept"), sem("pool_step"), sem("mix_made"), sem("pm_done"), sem("ssp_made"), sem("rp_done"),
            sem("pn_done"), sem("pool_hi"), sem("pool_lo"))
        lnm_made, ln_cent, ln_sq, lnv_made, ln_r, ln_y, ln_act, pw_made, oc_done, ssc_made, rc_done, cn_done, \
            conv_hi, conv_lo = (sem(n) for n in ("lnm_made", "ln_cent", "ln_sq", "lnv_made", "ln_r", "ln_y", "ln_act",
                                                 "pw_made", "oc_done", "ssc_made", "rc_done", "cn_done",
                                                 "conv_hi", "conv_lo"))
        v_kept, q_kept, k_kept, vt_made, vt_kept = (
            sem("v_kept"), sem("q_kept"), sem("k_kept"), sem("vt_made"), sem("vt_kept"))
        z_made, zm_done, log_step, sp_done, sum_made, lw_done, wt_done, o_made, o_sq, o_hi, o_acc, o_lo = (
            sem(n) for n in ("z_made", "zm_done", "log_step", "sp_done", "sum_made", "lw_done", "wt_done", "o_made",
                             "o_sq", "o_hi", "o_acc", "o_lo"))
        ssa_made, ra_done, t_done, y_done, y_sq, y_gain, y_acc = (
            sem(n) for n in ("ssa_made", "ra_done", "t_done", "y_done", "y_sq", "y_gain", "y_acc"))
        ssy_made, r1_done, th_done, h2_done, h2_hi, h2_lo, h2_sq, h2_acc, ss2_made, r2_done, rows_made, rows_kept = (
            sem(n) for n in ("ssy_made", "r1_done", "th_done", "h2_done", "h2_hi", "h2_lo", "h2_sq", "h2_acc",
                             "ss2_made", "r2_done", "rows_made", "rows_kept"))
        gs_done, silu_done, up_bank_free, p_done, f_hi, f_lo = (
            sem(n) for n in ("gs_done", "silu_done", "up_bank_free", "p_done", "f_hi", "f_lo"))
        down_free, dsq_done, f_done, sst_done, rd_done, res_done, exp_loaded = (
            sem(n) for n in ("down_free", "dsq_done", "f_done", "sst_done", "rd_done", "res_done", "exp_loaded"))

        def tiles(w):
            return w.rearrange("a (kt p) n -> p (a kt) n", p=P)

        win_v, wout_v, wg_v, wu_v, wd_v = tiles(w_in), tiles(w_out), tiles(w_gate), tiles(w_up), tiles(w_down)
        out_v = out.rearrange("a (m p) d -> p (a m) d", p=P)

        block = ctx.enter_context(nc.Block())

        @block.sync
        def _(sp_eng):
            for m in range(NQ):
                sp_eng.dma_start(xr[:, m, :], x[0, m * P:(m + 1) * P, :]).then_inc(x_landed, 16)
            sp_eng.dma_start(xr[0:META, 2, :], meta).then_inc(x_landed, 16)

            def load(src, kt, n0, q, slot, kts=CK, cols=BLK, wait=True):
                if wait:
                    sp_eng.wait_ge(lo_done, q - WSLOTS + 1)
                    if not isinstance(q, int):
                        sp_eng.sem_inc(slot_free, 1)
                sp_eng.dma_start(raw[:, slot, :].rearrange("p (k n) -> p k n", k=kts),
                                 src[:, kt:kt + kts, bass.ds(n0, cols)]).then_inc(raw_landed[slot], 16)

            for i in range(2):
                for b, col in enumerate((C_A, C_GATE)):
                    for s in range(CK):
                        q = Q_CONV + (2 * i + b) * CK + s
                        load(win_v, s * CK, col + i * BLK, q, s, wait=q >= WSLOTS)
            with sp_eng.Fori(0, 2) as i:
                for s in range(CK):
                    load(win_v, s * CK, C_POOL + i * BLK, i * CK + (Q_POOL + s), s)
            with sp_eng.Fori(0, GROUPS) as g:
                for b, col in enumerate((2 * DA, 0, DA)):
                    for s in range(CK):
                        load(win_v, s * CK, col + g * BLK, g * PER_G + (Q_ATT + b * CK + s), s)
            for n, (part, j) in enumerate(out_parts):
                for s in range(OC):
                    q = Q_OUT + n * OC + s
                    kt = (DA // P if part == "side" else 0) + s * CK
                    load(wout_v, kt, j * BLK, q, q % WSLOTS)
            with sp_eng.Fori(0, NFB) as i:
                for b, src in enumerate((wg_v, wu_v)):
                    for s in range(CK):
                        load(src, s * CK, i * BLK, i * 2 * CK + (Q_FFN + b * CK + s), s)
            with sp_eng.Fori(0, DN // 2) as i:
                for b in range(2):
                    for d in range(DCH):
                        load(wd_v, 2 * d, i * 2 * DCOLS + b * DCOLS, i * 2 * DCH + (Q_DOWN + b * DCH + d),
                             (b * DCH + d) % WSLOTS, kts=2, cols=DCOLS)
            for m in range(NQ):
                for n in range(2):
                    half = slice(n * D // 2, (n + 1) * D // 2)
                    sp_eng.wait_ge(res_done, 2 * m + n + 1)
                    sp_eng.dma_start(out_v[:, m, half], f_acc[:, m, half]).then_inc(stored, 16)
            sp_eng.wait_ge(stored, 16 * 2 * NQ)

        @block.gpsimd
        def _(pool):
            pool.memset(ident, 0.0).then_inc(const_step, 1)
            pool.memset(ones, 1.0).then_inc(const_step, 1)
            pool.memset(eps, EPS).then_inc(const_step, 1)
            pool.memset(negtri, -1.0).then_inc(const_step, 1)
            pool.memset(negones, -1.0).then_inc(const_step, 1)
            pool.memset(mask, 0.0).then_inc(const_step, 1)
            pool.wait_ge(const_step, 6)
            pool.affine_select(ident, ident, [[-1, P]], ALU.not_equal, 1.0, base=0,
                               channel_multiplier=1).then_inc(const_ready, 1)
            pool.affine_select(negtri, negtri, [[-1, P]], ALU.is_ge, 0.0, base=0,
                               channel_multiplier=1).then_inc(const_ready, 1)
            for at, n, base in ((S0, P - META, META), (S1, P, 0), (S2, TOK - 2 * P, 0)):
                pool.affine_select(mask[:, at:at + n], mask[:, at:at + n], [[1, n]], ALU.is_gt, NEG, base=base,
                                   channel_multiplier=-1).then_inc(const_ready, 1)
            pool.memset(glu[:, :, 0:GP], 0.0).then_inc(pads_ready, 1)
            pool.wait_ge(u_lo, KT)
            pool.wait_ge(pn_done, PT)
            pool.memset(kb[1][:, :, TOK:KPAD], 0.0).then_inc(pads_ready, 1)
            pool.memset(vb[1][:, :, TOK:KPAD], 0.0).then_inc(pads_ready, 1)

        def hi_view(ap):
            return ap.bitcast(F32)

        @block.scalar
        def _(act):
            def split_hi(q, slot, turn):
                act.wait_ge(raw_landed[slot], 16 * (turn + 1))
                if not isinstance(q, int) or q >= WSLOTS:
                    act.wait_ge(chunks_used, q - WSLOTS + 1)
                act.activation(w_hi[:, slot, :], raw[:, slot, :], ACT.Copy).then_inc(hi_done, 1)

            def split(q):
                split_hi(q, q % WSLOTS, q // WSLOTS)

            step = [0]

            def inv_rms(dst, src, n, done):
                act.activation(dst, src, ACT.Ln, bias=eps[0:dst.shape[0]], scale=1.0 / n).then_inc(log_step, 1)
                step[0] += 1
                act.wait_ge(log_step, step[0])
                act.activation(dst, dst, ACT.Exp, scale=-0.5).then_inc(done, 1)

            def rows(v):
                return v.rearrange("a (c p) -> (a c) p", p=P)

            at = 0
            for v in (pre_mix_g, mix_out_g, post_mix_g, pre_ffn_g, pool_scale, b_dw, conv_ln_g, conv_ln_b):
                n = v.shape[1] // P
                act.dma_start(vrow[at:at + n, :], rows(v)).then_inc(vec_landed, 16)
                at += n
            act.dma_start(drow[0:TAPS * CT, :], w_dw.rearrange("a w (c p) -> (a w c) p", p=P)).then_inc(vec_landed, 16)
            act.dma_start(wpl, w_pool.rearrange("a g c d -> c (a g) d")).then_inc(sw_landed, 16)
            act.dma_start(wpw, w_pw.rearrange("a (c p) n -> p (a c) n", p=P)).then_inc(sw_landed, 16)

            act.wait_ge(x_landed, 16 * 3)
            for m, n in ((0, P), (1, P), (2, META)):
                if m:
                    act.wait_ge(ss0_done, m)
                act.activation(junk[0:n], xr[0:n, m, :], ACT.Square, accum_out=ss0[0:n, m:m + 1]).then_inc(ss0_done, 1)
            act.wait_ge(const_step, 6)
            act.wait_ge(ss0_done, 3)
            inv_rms(r0[:, 0:2], ss0[:, 0:2], D, r0_done)
            inv_rms(r0[0:META, 2:3], ss0[0:META, 2:3], D, r0_done)
            act.wait_ge(vec_turned, 1)
            act.copy(vec, ps[:, 7, 0:NV]).then_inc(vec_done, 1)
            act.copy(dw, ps[:, 7, P:P + TAPS * CT]).then_inc(vec_done, 1)
            act.wait_ge(r0b_made, 1)
            act.copy(r0b, ps[:, 6, 0:TOK]).then_inc(r0b_done, 1)
            def keep_x(kt):
                act.wait_ge(xt_made, kt + 1)
                act.copy(xT[:, kt, :], ps[:, turn_bank[kt % 3], META:TOK]).then_inc(xt_kept, 1)

            keep_x(0)
            for kt in range(KT):
                if kt + 1 < KT:
                    keep_x(kt + 1)
                act.wait_ge(uf_done, kt + 1)
                act.copy(u[:, kt, 0, :], u_f[:, kt % 4, :]).then_inc(u_hi, 1)
                if kt % CK == CK - 1:
                    split(kt // CK)

            def soft(n):
                act.wait_ge(zm_done, n + 1)
                if n >= 1:
                    act.wait_ge(sp_done, n)
                act.activation(lg, zm[:, n % 2], ACT.Abs).then_inc(log_step, 1)
                step[0] += 1
                act.wait_ge(log_step, step[0])
                act.activation(lg, lg, ACT.Exp, scale=-1.0).then_inc(log_step, 1)
                step[0] += 1
                act.wait_ge(log_step, step[0])
                act.activation(lg, lg, ACT.Ln, bias=1.0).then_inc(lg_done, 1)

            def weights(n):
                act.wait_ge(lw_done, n + 1)
                if n >= 2:
                    act.wait_ge(o_made, n - 1)
                act.activation(wt[:, n % 2], lw[:, n % 2], ACT.Exp).then_inc(wt_done, 1)

            def head_pair_out(n):
                kt = n // 2
                o = ps[:, 7, (kt % 2) * SEQ:(kt % 2 + 1) * SEQ]
                act.wait_ge(o_made, n + 1)
                if kt >= 1:
                    act.wait_ge(o_acc, kt)
                act.activation(sq_o, o, ACT.Square).then_inc(o_sq, 1)
                act.activation(ffn[:, kt, 0, :], o, ACT.Copy, scale=vec[:, V_MIX + kt:V_MIX + kt + 1]).then_inc(o_hi, 1)

            for q in range(WSLOTS, Q_FFN + CK):
                split(q)
                e = q - 4
                for i in range(2):
                    if e == Q_CONV + 2 * i * CK + CK - 1:
                        act.wait_ge(chunks_used, e + 1)
                        if i:
                            act.wait_ge(glu_done, 1)
                        else:
                            act.wait_ge(u_lo, KT)
                        act.copy(a_s, ps[:, 0:2, 0:TOK]).then_inc(a_kept, 1)
                    if e == Q_CONV + 2 * i * CK + 2 * CK - 1:
                        act.wait_ge(chunks_used, e + 1)
                        act.activation(sg, ps[:, 2:4, 0:TOK], ACT.Sigmoid).then_inc(gate_sig, 1)
                    if e == Q_POOL + (i + 1) * CK - 1:
                        act.wait_ge(chunks_used, e + 1)
                        act.copy(pu[:, 2 * i:2 * i + 2, :], ps[:, 2 * i:2 * i + 2, 0:TOK]).then_inc(pu_kept, 1)
                if Q_ATT <= e < Q_OUT:
                    g, b = (e - Q_ATT) // PER_G, (e - Q_ATT) % PER_G
                    if b % CK == CK - 1:
                        act.wait_ge(chunks_used, e + 1)
                        if b < CK:
                            if g == 1:
                                act.wait_ge(pads_ready, 3)
                            if g >= 2:
                                act.wait_ge(vt_made, g - 1)
                            act.copy(vb[g % 2][:, :, 0:TOK], ps[:, 2:4, 0:TOK]).then_inc(v_kept, 1)
                        elif b < 2 * CK:
                            if g >= 2:
                                act.wait_ge(z_made, HPG * (g - 1))
                            act.mul(qb[g % 2], ps[:, 4, :].rearrange("p (m t) -> p m t", m=2),
                                    DH ** -0.5).then_inc(q_kept, 1)
                        else:
                            if g >= 2:
                                act.wait_ge(z_made, HPG * (g - 1))
                            act.copy(kb[g % 2][:, :, 0:TOK], ps[:, 0:2, 0:TOK]).then_inc(k_kept, 1)
                if q - LAG in VT_AT:
                    g = VT_AT[q - LAG]
                    act.wait_ge(vt_made, g + 1)
                    if g >= 2:
                        act.wait_ge(o_made, HPG * (g - 1))
                    for m in range(2):
                        act.copy(vT[g % 2][:, :, m * P:(m + 1) * P],
                                 ps[:, 5 + m, 0:KPAD].rearrange("p (k d) -> p k d", k=3)).then_inc(vt_kept, 1)
                if q - 5 in HEAD_AT:
                    weights(HEAD_AT[q - 5])
                if q - 3 in HEAD_AT:
                    soft(HEAD_AT[q - 3])
                if q - 7 in HEAD_AT and HEAD_AT[q - 7] % 2:
                    head_pair_out(HEAD_AT[q - 7])

                if q == PE_MIX + LAG:
                    act.wait_ge(mix_made, 1)
                    for g in range(NPG):
                        act.activation(mf[:, g, :], ps[:, 5 + g // 2, (g % 2) * SEQ:(g % 2 + 1) * SEQ], ACT.Copy,
                                       scale=vec[:, V_PS + g:V_PS + g + 1]).then_inc(pm_done, 1)
                    act.wait_ge(pm_done, NPG)
                    act.activation(sq4, mf, ACT.Square).then_inc(pm_done, 1)
                if q == PE_SSP + LAG:
                    act.wait_ge(ssp_made, 1)
                    inv_rms(rside, ps[:, 7, 0:SEQ], DP, rp_done)
                if q == PE_SSP + LAG + 1:
                    act.wait_ge(pn_done, PT)
                    act.copy(ffn[:, DA // P:DA // P + PT, 0, :], mf).then_inc(pool_hi, 1)

                if q == PE_LNM + LAG + 1:
                    act.wait_ge(ln_cent, CT)
                    act.activation(sq4, cy, ACT.Square).then_inc(ln_sq, 1)
                if q == PE_LNV + LAG:
                    act.wait_ge(lnv_made, 1)
                    act.wait_ge(pn_done, PT)
                    inv_rms(rside, ps[:, 0, 0:SEQ], DC, ln_r)
                if q == PE_LNV + LAG + 2:
                    act.wait_ge(ln_y, CT)
                    act.wait_ge(pool_lo, 1)
                    for t in range(CT):
                        act.activation(mf[:, t, :], cy[:, t, :], ACT.Silu,
                                       bias=vec[:, V_LNB + t:V_LNB + t + 1]).then_inc(ln_act, 1)
                if q == PE_PW + LAG + 1:
                    act.wait_ge(pw_made, 2)
                    act.copy(cy, ps[:, 0:2, :].rearrange("p b (c t) -> p (b c) t", c=2)).then_inc(oc_done, 1)
                    act.activation(sq4, ps[:, 0:2, :].rearrange("p b (c t) -> p (b c) t", c=2),
                                   ACT.Square).then_inc(oc_done, 1)
                if q == PE_SSC + LAG:
                    act.wait_ge(ssc_made, 1)
                    inv_rms(rside, ps[:, 2, 0:SEQ], DC, rc_done)
                if q == PE_SSC + LAG + 1:
                    act.wait_ge(cn_done, CT)
                    act.copy(ffn[:, (DA + DP) // P:KT, 0, :], mf).then_inc(conv_hi, 1)

                if q == PE_SSA + LAG:
                    act.wait_ge(ssa_made, 1)
                    inv_rms(ra[:, 0, :], ps[:, 7, 0:SEQ], DA, ra_done)
                    act.wait_ge(ra_done, 1)
                    act.copy(ra[:, 1, :], ra[:, 0, :]).then_inc(ra_done, 1)
                if q in OUT_EVAC:
                    j = OUT_EVAC[q]
                    act.wait_ge(y_done, j + 1)
                    if j >= 1:
                        act.wait_ge(y_acc, j)
                    act.activation(sqy, y[:, 2 * j:2 * j + 2, :], ACT.Square).then_inc(y_sq, 1)
                    act.wait_ge(y_sq, j + 1)
                    for kt in (2 * j, 2 * j + 1):
                        act.activation(y[:, kt, :], y[:, kt, :], ACT.Copy,
                                       scale=vec[:, V_POST + kt:V_POST + kt + 1]).then_inc(y_gain, 1)

            act.wait_ge(ssy_made, 1)
            inv_rms(r1[:, 0, :], ps[:, 1, 0:SEQ], D, r1_done)
            act.wait_ge(r1_done, 1)
            act.copy(r1[:, 1, :], r1[:, 0, :]).then_inc(r1_done, 1)
            for j in range(NOB):
                act.wait_ge(h2_done, j + 1)
                for kt in (2 * j, 2 * j + 1):
                    act.activation(u[:, kt, 0, 0:SEQ], xT[:, kt, :], ACT.Copy,
                                   scale=vec[:, V_FFN + kt:V_FFN + kt + 1]).then_inc(h2_hi, 1)
                act.activation(sqh[:, j, :], xT[:, 2 * j:2 * j + 2, :].rearrange("p a t -> p (a t)"),
                               ACT.Square).then_inc(h2_sq, 1)
                if j % 2 and j >= 3:
                    split(Q_FFN + CK + (j - 3) // 2)
            split(Q_FFN + 2 * CK - 1)
            act.wait_ge(ss2_made, 1)
            inv_rms(r2[:, 0, :], ps[:, 7, 0:SEQ], D, r2_done)
            act.wait_ge(r2_done, 1)
            act.copy(r2[:, 1, :], r2[:, 0, :]).then_inc(r2_done, 1)
            for n in range(2 * DN):
                act.wait_ge(rows_made, n + 1)
                act.copy(h2rows[:, n // DN, (n % DN) * DCOLS:(n % DN + 1) * DCOLS],
                         ps[:, 2 + n % 4, :]).then_inc(rows_kept, 1)
            act.wait_ge(rows_kept, 2 * DN)
            act.sem_inc(down_free, 4)
            act.dma_start(gbc[:, :], post_ffn_g.to_broadcast([P, D])).then_inc(gbc_landed, 16)

            def silu(i):
                act.wait_ge(gs_done, i + 1)
                act.activation(tmp_ffn[:, 1, :], tmp_ffn[:, 0, :], ACT.Silu).then_inc(silu_done, 1)

            silu0 = Q_FFN + 2 * CK
            with act.Fori(0, NFB - 1) as i:
                silu(i)
                for s in range(2 * CK):
                    split_hi(i * 2 * CK + (silu0 + s), s % WSLOTS, i * 2 + (silu0 + s) // WSLOTS)
            silu(NFB - 1)

            for q in range(Q_DOWN, Q_DOWN + DN * DCH + 4):
                if q < Q_DOWN + DN * DCH:
                    split(q)
                if q == Q_DOWN + 4:
                    act.activation(dummy, eps, ACT.Ln).then_inc(exp_loaded, 1)
                n, rest = (q - 4 - Q_DOWN) // DCH, (q - 4 - Q_DOWN) % DCH
                if q - 4 >= Q_DOWN and rest == DCH - 1:
                    act.wait_ge(chunks_used, q - 3)
                    for m in range(NQ):
                        if n or m:
                            act.wait_ge(dsq_done, NQ * n + m)
                        act.activation(tmp_ffn[:, 0, :], ps[:, 2 + 2 * (n % 2) + m, :], ACT.Square,
                                       accum_out=ssd[:, m, n:n + 1]).then_inc(dsq_done, 1)
                    act.wait_ge(dsq_done, NQ * (n + 1))
                    act.sem_inc(down_free, 1)
            act.wait_ge(sst_done, 1)
            inv_rms(rd, sst, D, rd_done)

        @block.vector
        def _(dve):
            def split_lo(q, slot):
                dve.wait_ge(hi_done, q + 1)
                dve.tensor_tensor(w_lo[:, slot, :], raw[:, slot, :], hi_view(w_hi[:, slot, :]),
                                  ALU.subtract).then_inc(lo_done, 1)

            def split(q):
                split_lo(q, q % WSLOTS)

            dve.wait_ge(const_ready, 1)
            dve.wait_ge(r0_done, 2)
            for m, n in ((0, P), (1, P), (2, META)):
                dve.tensor_scalar(diag[0:n, m, 0:n], ident[0:n, 0:n], r0[0:n, m:m + 1], None,
                                  ALU.mult).then_inc(diag_done, 1)
            dve.wait_ge(vec_done, 2)
            dve.wait_ge(r0b_done, 1)
            for kt in range(KT):
                dve.wait_ge(xt_kept, kt + 1)
                dve.scalar_tensor_tensor(u_f[:, kt % 4, :], ps[:, turn_bank[kt % 3], 0:TOK], vec[:, V_PRE + kt:V_PRE + kt + 1],
                                         r0b, ALU.mult, ALU.mult).then_inc(uf_done, 1)
                dve.wait_ge(u_hi, kt + 1)
                dve.tensor_tensor(u[:, kt, 1, :], u_f[:, kt % 4, :], hi_view(u[:, kt, 0, :]),
                                  ALU.subtract).then_inc(u_lo, 1)
                if kt % CK == CK - 1:
                    split(kt // CK)
            dve.wait_ge(u_lo, KT)
            dve.memset(kb[0][:, :, TOK:KPAD], 0.0).then_inc(pads0, 1)
            dve.memset(vb[0][:, :, TOK:KPAD], 0.0).then_inc(pads0, 1)

            def masked(n):
                dve.wait_ge(z_made, n + 1)
                dve.tensor_tensor(zm[:, n % 2], ps[:, 5 + n % 2, 0:SM], mask, ALU.add).then_inc(zm_done, 1)

            def softplus(n):
                dve.wait_ge(lg_done, n + 1)
                dve.scalar_tensor_tensor(sp[:, n % 2], zm[:, n % 2], 0.0, lg, ALU.max, ALU.add).then_inc(sp_done, 1)

            def log_weights(n):
                dve.wait_ge(sum_made, n + 1)
                if n >= 2:
                    dve.wait_ge(wt_done, n - 1)
                dve.scalar_tensor_tensor(lw[:, n % 2], ps[:, 5 + n % 2, 0:SM], 0.0, mask,
                                         ALU.min, ALU.add).then_inc(lw_done, 1)

            def head_pair_out(n):
                kt = n // 2
                dve.wait_ge(o_hi, kt + 1)
                dve.scalar_tensor_tensor(ffn[:, kt, 1, :], ps[:, 7, (kt % 2) * SEQ:(kt % 2 + 1) * SEQ],
                                         vec[:, V_MIX + kt:V_MIX + kt + 1], hi_view(ffn[:, kt, 0, :]),
                                         ALU.mult, ALU.subtract).then_inc(o_lo, 1)
                dve.wait_ge(o_sq, kt + 1)
                if kt == 0:
                    dve.tensor_copy(acc_o, sq_o).then_inc(o_acc, 1)
                else:
                    dve.wait_ge(o_acc, kt)
                    dve.tensor_tensor(acc_o, acc_o, sq_o, ALU.add).then_inc(o_acc, 1)

            for q in range(WSLOTS, Q_FFN + CK):
                split(q)
                if q - 5 in HEAD_AT:
                    log_weights(HEAD_AT[q - 5])
                if q - 4 in HEAD_AT:
                    softplus(HEAD_AT[q - 4])
                if q - 3 in HEAD_AT:
                    masked(HEAD_AT[q - 3])
                if q - 7 in HEAD_AT and HEAD_AT[q - 7] % 2:
                    head_pair_out(HEAD_AT[q - 7])
                for i in range(2):
                    if q - 4 == Q_CONV + 2 * i * CK + 2 * CK - 1:
                        dve.wait_ge(a_kept, i + 1)
                        dve.wait_ge(gate_sig, i + 1)
                        dve.tensor_tensor(glu[:, 2 * i:2 * i + 2, GP:GP + TOK], a_s, sg, ALU.mult).then_inc(glu_done, 1)
                w = q - Q_TAPS
                if 0 <= w < TAPS:
                    if w == 0:
                        dve.wait_ge(pads_ready, 1)
                        dve.wait_ge(glu_done, 2)
                    for t in range(CT):
                        src = glu[:, t, META + w:META + w + SEQ]
                        tap = dw[:, w * CT + t:w * CT + t + 1]
                        if w == 0:
                            dve.tensor_scalar(cy[:, t, :], src, tap, vec[:, V_BDW + t:V_BDW + t + 1],
                                              ALU.mult, ALU.add).then_inc(tap_done, 1)
                        else:
                            dve.wait_ge(tap_done, (w - 1) * CT + t + 1)
                            dve.scalar_tensor_tensor(cy[:, t, :], src, tap, cy[:, t, :],
                                                     ALU.mult, ALU.add).then_inc(tap_done, 1)
                if q == Q_POOL + 2 * CK + LAG + 1:
                    dve.wait_ge(pu_kept, 2)
                    src = pu
                    for n in range(NPG):
                        d = 1 << n
                        lo = 2 * d - 1
                        dst = (pw0, pw1)[n % 2]
                        dve.tensor_tensor(dst[:, n:NPG, lo:TOK], src[:, n:NPG, lo:TOK], src[:, n:NPG, lo - d:TOK - d],
                                          ALU.add).then_inc(pool_step, 1)
                        dve.wait_ge(pool_step, 2 * n + 1)
                        dve.scalar_tensor_tensor(pooled[:, n, :], dst[:, n, META:TOK], 1.0 / (2 * d), pu[:, n, META:TOK],
                                                 ALU.mult, ALU.subtract).then_inc(pool_step, 1)
                        src = dst
                if q == PE_SSP + LAG:
                    dve.wait_ge(rp_done, 1)
                    for t in range(PT):
                        g = V_MIX + DA // P + t
                        dve.scalar_tensor_tensor(mf[:, t, :], mf[:, t, :], vec[:, g:g + 1], rside,
                                                 ALU.mult, ALU.mult).then_inc(pn_done, 1)
                if q == PE_SSP + LAG + 1:
                    dve.wait_ge(pool_hi, 1)
                    at = DA // P
                    dve.tensor_tensor(ffn[:, at:at + PT, 1, :], mf, hi_view(ffn[:, at:at + PT, 0, :]),
                                      ALU.subtract).then_inc(pool_lo, 1)
                if q == PE_LNM + LAG:
                    dve.wait_ge(lnm_made, 1)
                    for t in range(CT):
                        dve.scalar_tensor_tensor(cy[:, t, :], ps[:, 0, 0:SEQ], -1.0 / DC, cy[:, t, :],
                                                 ALU.mult, ALU.add).then_inc(ln_cent, 1)
                if q == PE_LNV + LAG + 1:
                    dve.wait_ge(ln_r, 1)
                    for t in range(CT):
                        dve.scalar_tensor_tensor(cy[:, t, :], cy[:, t, :], vec[:, V_LNG + t:V_LNG + t + 1], rside,
                                                 ALU.mult, ALU.mult).then_inc(ln_y, 1)
                if q == PE_SSC + LAG:
                    dve.wait_ge(rc_done, 1)
                    for t in range(CT):
                        g = V_MIX + (DA + DP) // P + t
                        dve.scalar_tensor_tensor(mf[:, t, :], cy[:, t, :], vec[:, g:g + 1], rside,
                                                 ALU.mult, ALU.mult).then_inc(cn_done, 1)
                if q == PE_SSC + LAG + 1:
                    dve.wait_ge(conv_hi, 1)
                    at = (DA + DP) // P
                    dve.tensor_tensor(ffn[:, at:KT, 1, :], mf, hi_view(ffn[:, at:KT, 0, :]),
                                      ALU.subtract).then_inc(conv_lo, 1)
                if q in OUT_EVAC:
                    j = OUT_EVAC[q]
                    dve.wait_ge(chunks_used, q - 3)
                    dve.wait_ge(ra_done, 2)
                    dve.tensor_tensor(tb, ps[:, attn_bank[j], :].rearrange("p (m t) -> p m t", m=2), ra,
                                      ALU.mult).then_inc(t_done, 1)
                    dve.wait_ge(t_done, j + 1)
                    dve.tensor_tensor(y[:, 2 * j:2 * j + 2, :], tb,
                                      ps[:, side_bank[j], :].rearrange("p (m t) -> p m t", m=2),
                                      ALU.add).then_inc(y_done, 1)
                    dve.wait_ge(y_sq, j + 1)
                    if j == 0:
                        dve.tensor_copy(accy, sqy).then_inc(y_acc, 1)
                    else:
                        dve.wait_ge(y_acc, j)
                        dve.tensor_tensor(accy, accy, sqy, ALU.add).then_inc(y_acc, 1)

            dve.wait_ge(r1_done, 2)
            dve.wait_ge(y_gain, KT)
            for j in range(NOB):
                pair = slice(2 * j, 2 * j + 2)
                if j >= 2:
                    dve.wait_ge(h2_done, j - 1)
                dve.tensor_tensor(th[:, j % 2], y[:, pair, :], r1, ALU.mult).then_inc(th_done, 1)
                dve.wait_ge(th_done, j + 1)
                dve.tensor_tensor(xT[:, pair, :], th[:, j % 2], xT[:, pair, :], ALU.add).then_inc(h2_done, 1)
                for kt in (2 * j, 2 * j + 1):
                    dve.wait_ge(h2_hi, kt + 1)
                    dve.scalar_tensor_tensor(u[:, kt, 1, 0:SEQ], xT[:, kt, :], vec[:, V_FFN + kt:V_FFN + kt + 1],
                                             hi_view(u[:, kt, 0, 0:SEQ]), ALU.mult, ALU.subtract).then_inc(h2_lo, 1)
                if j % 2 and j >= 3:
                    split(Q_FFN + CK + (j - 3) // 2)
            acc2 = accy.rearrange("p a t -> p (a t)")
            for j in range(1, NOB):
                dve.wait_ge(h2_sq, j + 1)
                if j >= 2:
                    dve.wait_ge(h2_acc, j - 1)
                dve.tensor_tensor(acc2, sqh[:, 0, :] if j == 1 else acc2, sqh[:, j, :], ALU.add).then_inc(h2_acc, 1)
            split(Q_FFN + 2 * CK - 1)

            r2f = r2.rearrange("p a t -> p (a t)")

            def gate_evac(i):
                dve.wait_ge(chunks_used, i * 2 * CK + (Q_FFN + CK))
                dve.tensor_tensor(tmp_ffn[:, 0, :], ps[:, 0, :], r2f, ALU.mult).then_inc(gs_done, 1)

            def up_evac(i):
                dve.wait_ge(chunks_used, i * 2 * CK + (Q_FFN + 2 * CK))
                dve.tensor_tensor(tmp_ffn[:, 2, :], ps[:, 1, :], r2f, ALU.mult).then_inc(up_bank_free, 1)
                dve.wait_ge(silu_done, i + 1)
                dve.wait_ge(up_bank_free, i + 2)
                dve.tensor_tensor(tmp_ffn[:, 3, :], tmp_ffn[:, 1, :], tmp_ffn[:, 2, :], ALU.mult).then_inc(p_done, 1)
                sl, us, p = (tmp_ffn[:, n, :].rearrange("p (a t) -> p a t", a=2) for n in (1, 2, 3))
                dve.tensor_tensor(ffn[:, bass.ds(2 * i, 2), 0, :], sl, us, ALU.mult).then_inc(f_hi, 1)
                dve.wait_ge(f_hi, i + 1)
                dve.wait_ge(p_done, i + 1)
                dve.tensor_tensor(ffn[:, bass.ds(2 * i, 2), 1, :], p, hi_view(ffn[:, bass.ds(2 * i, 2), 0, :]),
                                  ALU.subtract).then_inc(f_lo, 1)

            dve.wait_ge(r2_done, 2)
            dve.sem_inc(up_bank_free, 1)
            dve.wait_ge(rows_made, 2 * DN)
            with dve.Fori(0, NFB - 1) as i:
                gate_evac(i)
                for s in range(CK):
                    split_lo(i * 2 * CK + (Q_FFN + 2 * CK + s), s)
                up_evac(i)
                for s in range(CK):
                    split_lo(i * 2 * CK + (Q_FFN + 3 * CK + s), s)
            gate_evac(NFB - 1)
            for q in range(Q_DOWN, Q_DOWN + DN * DCH + 4):
                if q < Q_DOWN + DN * DCH:
                    split(q)
                if q == Q_DOWN + 3:
                    up_evac(NFB - 1)
                n, rest = (q - 4 - Q_DOWN) // DCH, (q - 4 - Q_DOWN) % DCH
                if q - 4 >= Q_DOWN and rest == DCH - 1:
                    cols = slice(n * DCOLS, (n + 1) * DCOLS)
                    dve.wait_ge(chunks_used, q - 3)
                    if n == 0:
                        dve.wait_ge(gbc_landed, 16)
                    for m in range(NQ):
                        dve.wait_ge(dsq_done, NQ * n + m + 1)
                        dve.tensor_tensor(f_acc[:, m, cols], ps[:, 2 + 2 * (n % 2) + m, :], gbc[:, cols],
                                          ALU.mult).then_inc(f_done, 1)
                    dve.wait_ge(f_done, NQ * (n + 1))
                    dve.sem_inc(down_free, 1)
            dve.wait_ge(dsq_done, NQ * DN)
            dve.tensor_reduce(sst, ssd, AX.X, ALU.add).then_inc(sst_done, 1)
            dve.wait_ge(rd_done, 1)
            for m in range(NQ):
                for n in range(2):
                    half = slice(n * D // 2, (n + 1) * D // 2)
                    dve.scalar_tensor_tensor(f_acc[:, m, half], f_acc[:, m, half], rd[:, m:m + 1],
                                             h2rows[:, m, half], ALU.mult, ALU.add).then_inc(res_done, 1)

        @block.tensor
        def _(pe):
            def products(q, slot, kts, rhs, outs, first, last, one_bank):
                pe.wait_ge(lo_done, q + 1)
                for k, kt in enumerate(kts):
                    x_hi, x_lo = rhs(kt)
                    for m in range(2):
                        at = slice(k * BLK + m * P, k * BLK + (m + 1) * P)
                        start = first and k == 0
                        pe.matmul(outs[m], w_hi[:, slot, at], x_hi, start=start and not (one_bank and m), stop=False,
                                  skip_group_check=True)
                        pe.matmul(outs[m], w_hi[:, slot, at], x_lo, start=False, stop=False, skip_group_check=True)
                        mm = pe.matmul(outs[m], w_lo[:, slot, at], x_hi, start=False,
                                       stop=last and k == len(kts) - 1, skip_group_check=True)
                mm.then_inc(chunks_used, 1)

            def normed(kt, lo=0):
                return u[:, kt, 0, lo:TOK], u[:, kt, 1, lo:TOK]

            def ffn_input(kt):
                return u[:, kt, 0, 0:SEQ], u[:, kt, 1, 0:SEQ]

            def merged(kt):
                return ffn[:, kt, 0, :], ffn[:, kt, 1, :]

            def two(bank):
                return [ps[:, bank, 0:SEQ], ps[:, bank, SEQ:2 * SEQ]]

            def wide(bank):
                return [ps[:, bank, 0:TOK], ps[:, bank + 1, 0:TOK]]

            def column_sums(dst, srcs, made):
                for n, s in enumerate(srcs):
                    mm = pe.matmul(dst, ones, s, start=n == 0, stop=n == len(srcs) - 1)
                mm.then_inc(made, 1)

            pe.wait_ge(const_ready, 1)
            pe.wait_ge(vec_landed, 16 * 9)
            pe.transpose(ps[:, 7, 0:NV], vrow[0:NV, :], ident[0:NV, 0:NV])
            pe.transpose(ps[:, 7, P:P + TAPS * CT], drow[0:TAPS * CT, :],
                         ident[0:TAPS * CT, 0:TAPS * CT]).then_inc(vec_turned, 1)
            pe.wait_ge(x_landed, 16 * 3)

            def turn(kt):
                b = turn_bank[kt % 3]
                if kt == 2:
                    pe.wait_ge(vec_done, 2)
                if kt >= 3:
                    pe.wait_ge(uf_done, kt - 2)
                cols = slice(kt * P, (kt + 1) * P)
                pe.transpose(ps[:, b, 0:META], xr[0:META, 2, cols], ident[0:META, 0:META])
                pe.transpose(ps[:, b, META:META + P], xr[:, 0, cols], ident)
                pe.transpose(ps[:, b, META + P:TOK], xr[:, 1, cols], ident).then_inc(xt_made, 1)

            turn(0)
            turn(1)
            pe.wait_ge(const_step, 6)
            pe.wait_ge(diag_done, 3)
            pe.matmul(ps[:, 6, 0:META], ones[0:META, :], diag[0:META, 2, 0:META], start=True, stop=True)
            pe.matmul(ps[:, 6, META:META + P], ones, diag[:, 0, :], start=True, stop=True)
            pe.matmul(ps[:, 6, META + P:TOK], ones, diag[:, 1, :], start=True, stop=True).then_inc(r0b_made, 1)
            for kt in range(2, KT):
                turn(kt)

            def proj(q0, outs, one_bank=False, lo=0):
                for s in range(CK):
                    pe.wait_ge(u_lo, (s + 1) * CK)
                    products(q0 + s, s, range(s * CK, (s + 1) * CK), lambda kt: normed(kt, lo), outs,
                             s == 0, s == CK - 1, one_bank)

            for i in range(2):
                if i:
                    pe.wait_ge(a_kept, i)
                proj(i * 2 * CK + Q_CONV, wide(0))
                if i:
                    pe.wait_ge(gate_sig, i)
                proj(i * 2 * CK + (Q_CONV + CK), wide(2))
            pe.wait_ge(a_kept, 2)
            proj(Q_POOL, wide(0))
            pe.wait_ge(gate_sig, 2)
            proj(Q_POOL + CK, wide(2))

            tiles_of = ((S0, META), (S1, P), (S2, 2 * P))

            def scores(n):
                g, t, half = n // HPG, n % HPG // 2, slice(n % 2 * DH, n % 2 * DH + DH)
                z = ps[:, 5 + n % 2, :]
                pe.wait_ge(k_kept, g + 1)
                pe.wait_ge(q_kept, g + 1)
                if g == 0:
                    pe.wait_ge(pads0, 2)
                if n >= 2:
                    pe.wait_ge(lw_done, n - 1)
                pe.wait_ge(vt_kept, 2 * (g + 1))
                for k, (at, t0) in enumerate(tiles_of):
                    mm = pe.matmul(z[:, at:at + TOK - t0], kb[g % 2][half, t, k * P:(k + 1) * P],
                                   qb[g % 2][half, t, t0 - META:SEQ], start=k == 0, stop=k == 2, skip_group_check=True)
                mm.then_inc(z_made, 1)

            def later_sums(n):
                z, s = ps[:, 5 + n % 2, :], sp[:, n % 2]
                pe.wait_ge(sp_done, n + 1)
                if n == 0:
                    pe.wait_ge(const_ready, 2)
                pe.matmul(z[:, 0:SM], negtri, s[:, 0:SM], start=False, stop=False, skip_group_check=True)
                pe.matmul(z[:, P - META:SEQ], negones, s[:, S1:S2], start=False, stop=False, skip_group_check=True)
                pe.matmul(z[:, S1 + P:S2], negones, s[:, S2:SM], start=False, stop=False, skip_group_check=True)
                pe.matmul(z[:, 2 * P - META:SEQ], negones, s[:, S2:SM], start=False, stop=True,
                          skip_group_check=True).then_inc(sum_made, 1)

            def values(n):
                g, t, e = n // HPG, n % HPG // 2, n % 2
                pe.wait_ge(wt_done, n + 1)
                if n % 2 == 0 and n >= 2:
                    pe.wait_ge(o_lo, n // 2)
                o = ps[e * DH:(e + 1) * DH, 7, t * SEQ:(t + 1) * SEQ]
                for k, (at, t0) in enumerate(tiles_of):
                    mm = pe.matmul(o[:, t0 - META:SEQ], vT[g % 2][:, k, t * P + e * DH:t * P + (e + 1) * DH],
                                   wt[:, n % 2, at:at + TOK - t0], start=k == 0, stop=k == 2, skip_group_check=True)
                mm.then_inc(o_made, 1)

            def side_work(q):
                if q - 4 in HEAD_AT:
                    values(HEAD_AT[q - 4])
                if q - 2 in HEAD_AT:
                    later_sums(HEAD_AT[q - 2])
                if q in HEAD_AT:
                    scores(HEAD_AT[q])
                if q in VT_AT:
                    g = VT_AT[q]
                    pe.wait_ge(v_kept, g + 1)
                    if g == 0:
                        pe.wait_ge(pm_done, NPG + 1)
                        pe.wait_ge(pads0, 2)
                    else:
                        pe.wait_ge(lw_done, HPG * g)
                    for m in range(2):
                        for k in range(3):
                            mm = pe.transpose(ps[:, 5 + m, k * P:(k + 1) * P], vb[g % 2][:, m, k * P:(k + 1) * P], ident)
                    mm.then_inc(vt_made, 1)
                if q == PE_MIX:
                    pe.wait_ge(sw_landed, 32)
                    pe.wait_ge(pool_step, 2 * NPG)
                    for g in range(NPG):
                        mm = pe.matmul(ps[:, 5 + g // 2, (g % 2) * SEQ:(g % 2 + 1) * SEQ], wpl[:, g, :],
                                       pooled[:, g, :], start=True, stop=True)
                    mm.then_inc(mix_made, 1)
                if q == PE_SSP:
                    pe.wait_ge(pm_done, NPG + 1)
                    column_sums(ps[:, 7, 0:SEQ], [sq4[:, t, :] for t in range(PT)], ssp_made)
                if q == PE_LNM:
                    pe.wait_ge(tap_done, TAPS * CT)
                    pe.wait_ge(k_kept, (q - SC) // PER_G + 1)
                    column_sums(ps[:, 0, 0:SEQ], [cy[:, t, :] for t in range(CT)], lnm_made)
                if q == PE_LNV:
                    pe.wait_ge(ln_sq, 1)
                    column_sums(ps[:, 0, 0:SEQ], [sq4[:, t, :] for t in range(CT)], lnv_made)
                if q in (PE_PW, PE_PW + 1):
                    b = q - PE_PW
                    pe.wait_ge(ln_act, CT)
                    pe.wait_ge(k_kept, (PE_PW - SC) // PER_G + 1)
                    for m in range(2):
                        d0 = (2 * b + m) * P
                        for t in range(CT):
                            mm = pe.matmul(ps[:, b, m * SEQ:(m + 1) * SEQ], wpw[:, t, d0:d0 + P], mf[:, t, :],
                                           start=t == 0, stop=t == CT - 1)
                    mm.then_inc(pw_made, 1)
                if q == PE_SSC:
                    pe.wait_ge(oc_done, 2)
                    pe.wait_ge(v_kept, GROUPS)
                    column_sums(ps[:, 2, 0:SEQ], [sq4[:, t, :] for t in range(CT)], ssc_made)
                if q == PE_SSA:
                    pe.wait_ge(o_acc, DA // P)
                    pe.wait_ge(o_lo, DA // P)
                    column_sums(ps[:, 7, 0:SEQ], [acc_o], ssa_made)

            for g in range(GROUPS):
                for b, outs in enumerate((wide(2), two(4), wide(0))):
                    q0 = Q_ATT + g * PER_G + b * CK
                    if b == 0:
                        pe.wait_ge(pu_kept, 2)
                        if g:
                            pe.wait_ge(v_kept, g)
                    if b == 1:
                        pe.wait_ge(xt_kept, KT)
                        if g:
                            pe.wait_ge(q_kept, g)
                    if b == 2 and g:
                        pe.wait_ge(k_kept, g)
                    if b == 2 and q0 > PE_PW:
                        pe.wait_ge(oc_done, 2)
                    if b == 2 and PE_LNV < q0 < PE_PW:
                        pe.wait_ge(ln_r, 1)
                    for s in range(CK):
                        side_work(q0 + s)
                        lo = META if b == 1 else 0
                        products(q0 + s, s, range(s * CK, (s + 1) * CK), lambda kt: normed(kt, lo), outs,
                                 s == 0, s == CK - 1, b == 1)

            y_of = {}
            for n, (part, j) in enumerate(out_parts):
                bank = (side_bank if part == "side" else attn_bank)[j]
                kt0 = DA // P if part == "side" else 0
                for s in range(OC):
                    q = Q_OUT + n * OC + s
                    side_work(q)
                    if s == 0:
                        if bank in y_of:
                            pe.wait_ge(y_done, y_of[bank] + 1)
                        elif part == "side":
                            pe.wait_ge((k_kept, k_kept, rc_done, v_kept, q_kept)[bank],
                                       (GROUPS, GROUPS, 1, GROUPS, GROUPS)[bank])
                        elif bank == 7:
                            pe.wait_ge(ra_done, 1)
                        else:
                            pe.wait_ge(lw_done, NH)
                        y_of[bank] = j
                    if part == "side":
                        pe.wait_ge(pool_lo, 1)
                        if s:
                            pe.wait_ge(conv_lo, 1)
                    else:
                        pe.wait_ge(o_lo, (s + 1) * CK)
                    products(q, q % WSLOTS, range(kt0 + s * CK, kt0 + (s + 1) * CK), merged, two(bank),
                             s == 0, s == OC - 1, True)

            pe.wait_ge(y_acc, NOB)
            column_sums(ps[:, 1, 0:SEQ], [accy[:, 0, :], accy[:, 1, :]], ssy_made)
            for s in range(CK):
                pe.wait_ge(h2_lo, (s + 1) * CK)
                products(Q_FFN + s, s, range(s * CK, (s + 1) * CK), ffn_input, two(0), s == 0, s == CK - 1, True)
            pe.wait_ge(h2_acc, NOB - 1)
            column_sums(ps[:, 7, 0:SEQ], [accy[:, 0, :], accy[:, 1, :]], ss2_made)
            for n in range(2 * DN):
                m = n // DN
                if n >= 4:
                    pe.wait_ge(rows_kept, n - 3)
                for k in range(4):
                    kt = n % DN * 4 + k
                    mm = pe.transpose(ps[:, 2 + n % 4, k * P:(k + 1) * P], xT[:, kt, m * P:(m + 1) * P], ident)
                mm.then_inc(rows_made, 1)
            pe.wait_ge(r1_done, 1)

            def ffn_block(q0, bank):
                for s in range(CK):
                    products(q0 + s, s, range(s * CK, (s + 1) * CK), ffn_input, two(bank), s == 0, s == CK - 1, True)

            with pe.Fori(0, NFB - 1) as i:
                pe.wait_ge(up_bank_free, i + 1)
                ffn_block(i * 2 * CK + (Q_FFN + CK), 1)
                pe.wait_ge(gs_done, i + 1)
                ffn_block(i * 2 * CK + (Q_FFN + 2 * CK), 0)
            pe.wait_ge(up_bank_free, NFB)
            ffn_block(Q_FFN + 2 * CK * NFB - CK, 1)

            with pe.Fori(0, DN // 2) as i:
                for b in range(2):
                    pe.wait_ge(down_free, i * 4 + (2 * b + 2))
                    for d in range(DCH):
                        slot = (b * DCH + d) % WSLOTS
                        pe.wait_ge(lo_done, i * 2 * DCH + (Q_DOWN + b * DCH + d + 1))
                        pe.wait_ge(f_lo, d + 1)
                        for k in range(2):
                            kt = 2 * d + k
                            mv = slice(k * DCOLS, (k + 1) * DCOLS)
                            for m in range(NQ):
                                o = ps[:, 2 + 2 * b + m, :]
                                rows_m = slice(m * P, (m + 1) * P)
                                first, last = d == 0 and k == 0, d == DCH - 1 and k == 1
                                pe.matmul(o, ffn[:, kt, 0, rows_m], w_hi[:, slot, mv], start=first, stop=False)
                                pe.matmul(o, ffn[:, kt, 0, rows_m], w_lo[:, slot, mv], start=False, stop=False)
                                mm = pe.matmul(o, ffn[:, kt, 1, rows_m], w_hi[:, slot, mv], start=False, stop=last)
                        mm.then_inc(chunks_used, 1)


_INS = ['x', 'meta_tokens', 'pre_mix_g', 'w_in', 'w_pool', 'pool_scale', 'w_dw', 'b_dw', 'conv_ln_g', 'conv_ln_b',
        'w_pw', 'mix_out_g', 'w_out', 'post_mix_g', 'pre_ffn_g', 'w_gate', 'w_up', 'w_down', 'post_ffn_g']


def kernel(**inputs):
    import numpy as np
    import concourse.bacc as bacc
    from concourse.bass_utils import run_bass_kernel_spmd

    nc = bacc.Bacc("TRN2", target_bir_lowering=False, num_devices=1)
    arrays, args = {}, []
    for name in _INS:
        a = np.ascontiguousarray(inputs[name])
        arrays[f"in_{name}"] = a
        args.append(nc.dram_tensor(f"in_{name}", a.shape, mybir.dt.from_np(a.dtype), kind="ExternalInput").ap())
    out = nc.dram_tensor("out", inputs["x"].shape, F32, kind="ExternalOutput").ap()
    build_trunk(nc, *args, out)
    r = run_bass_kernel_spmd(nc, [arrays], core_ids=[0])
    return r.results[0]["out"]
```

```python
from contextlib import ExitStack

import concourse.bass as bass
from concourse import mybir

F32 = mybir.dt.float32
F32R = mybir.dt.float32r
ALU = mybir.AluOpType
ACT = mybir.ActivationFunctionType
AX = mybir.AxisListType

P = 128
EPS = 1e-6
NEG = -1e30
WSLOTS = 4
CK = 4
BLK = 256
DCOLS = 512
LAG = 3


def build_trunk(nc, x, meta, pre_mix_g, w_in, w_pool, pool_scale, w_dw, b_dw, conv_ln_g, conv_ln_b, w_pw,
                mix_out_g, w_out, post_mix_g, pre_ffn_g, w_gate, w_up, w_down, post_ffn_g, out):
    _, SEQ, D = x.shape
    META = meta.shape[0]
    TOK = META + SEQ
    NQ = SEQ // P
    KT = D // P
    TAPS, DC = w_dw.shape[1], w_dw.shape[2]
    NPG, PG = w_pool.shape[1], w_pool.shape[2]
    DP = NPG * PG
    DA = D - DP - DC
    DH = 64
    FF = w_gate.shape[2]
    FT = FF // P
    CT = DC // P
    PT = DP // P
    KPAD = 3 * P
    GROUPS = DA // BLK
    HPG = BLK // DH
    assert NQ == 2 and P < TOK - P and TOK <= KPAD and PG == P

    Q_CONV = 0
    Q_POOL = Q_CONV + 4 * CK
    Q_ATT = Q_POOL + 2 * CK
    PER_G = 3 * CK
    Q_OUT = Q_ATT + GROUPS * PER_G
    FIRST = 5
    NOB = D // BLK
    Q_FFN = Q_OUT + NOB * CK
    NFB = FF // BLK
    Q_DOWN = Q_FFN + 2 * CK * NFB
    DN = D // DCOLS
    DCH = FT // 2
    SC = (Q_ATT + PER_G)
    C_POOL, C_A, C_GATE = 3 * DA, 3 * DA + DP, 3 * DA + DP + DC

    def attn_at(n):
        g, h = n // HPG, n % HPG
        if g == GROUPS - 1:
            return Q_OUT + 1 + h + h // 2
        return SC + PER_G * g + 1 + 2 * h
    NH = GROUPS * HPG
    HEAD_AT = {attn_at(n): n for n in range(NH)}
    VT_AT = {SC + PER_G * g - 1: g for g in range(GROUPS)}
    Q_TAPS = Q_POOL + CK
    VEC_AT, TURN_AT = 3, 4
    PE_MIX = Q_POOL + 14
    PE_SSP = Q_POOL + 18
    PE_LNM = Q_TAPS + TAPS - 1
    PE_LNV = PE_LNM + 4
    PE_PW = PE_LNV + 9
    PE_SSC = PE_PW + 6
    PE_SSA = Q_OUT + 12

    out_parts = [("side", j) for j in range(FIRST)] + [("attn", j) for j in range(FIRST)] + \
                [("side", j) for j in range(FIRST, NOB)] + [("attn", j) for j in range(FIRST, NOB)]
    OC = CK // 2
    side_bank = [4, 3, 2, 0, 1, 2, 0, 1]
    attn_bank = [5, 6, 7, 4, 3, 5, 6, 7]
    pool_bank = [0, 5]
    OUT_EVAC = {Q_OUT + OC * n + OC - 1 + 4: j for n, (part, j) in enumerate(out_parts) if part == "attn"}

    with ExitStack() as ctx:
        top = [(nc.sbuf_base + 63) // 64 * 64]

        def place(nbytes):
            at = top[0]
            top[0] += nbytes
            return at

        def sb_at(name, shape, dt, at):
            return nc.alloc_sbuf_tensor_at(name, shape, dt, offset=at)

        CE = CK * BLK
        raw = sb_at("raw", [P, WSLOTS, CE], F32, place(4 * WSLOTS * CE))
        w_hi = sb_at("w_hi", [P, WSLOTS, CE], F32R, place(4 * WSLOTS * CE))
        w_lo = sb_at("w_lo", [P, WSLOTS, CE], F32R, place(4 * WSLOTS * CE))
        a_in = place(4 * KT * 2 * TOK)
        u = sb_at("u", [P, KT, 2, TOK], F32R, a_in)
        f_acc = sb_at("f_acc", [P, NQ, D], F32, a_in)
        a_xt = place(4 * KT * SEQ)
        xT = sb_at("xT", [P, KT, SEQ], F32, a_xt)
        gbc = sb_at("gbc", [P, D], F32, a_xt)
        tmp_ffn = sb_at("tmp_ffn", [P, 4, 2 * SEQ], F32, a_xt + 4 * D)
        xs = sb_at("xs", [P, NQ, D], F32, a_xt)
        a_y = place(4 * KT * SEQ)
        y = sb_at("y", [P, KT, SEQ], F32, a_y)
        h2rows = sb_at("h2rows", [P, NQ, D], F32, a_y)
        side = sb_at("side", [P, KT * SEQ], F32, a_y)
        a_c = place(4 * 1152)
        cst = sb_at("cst", [P, 1152], F32, a_c)
        a_ff = place(4 * FT * 2 * SEQ)
        ffn = sb_at("ffn", [P, FT, 2, SEQ], F32R, a_ff)
        AR = (FT - KT) * 2 * SEQ
        arena = sb_at("arena", [P, AR], F32, a_ff + 4 * KT * 2 * SEQ)
        assert top[0] <= nc.sbuf_usable_end

        def carve(tensor, at, *dims):
            n = 1
            for d in dims:
                n *= d
            ap = tensor[:, at:at + n]
            if len(dims) == 2:
                ap = ap.rearrange("p (a b) -> p a b", a=dims[0])
            if len(dims) == 3:
                ap = ap.rearrange("p (a b c) -> p a b c", a=dims[0], b=dims[1])
            return ap, at + n

        ident, c = carve(cst, 0, P)
        ones, c = carve(cst, c, P)
        NV = 4 * KT + PT + 3 * CT
        NB = NV - KT
        vec, c = carve(cst, c, NV)
        dw, c = carve(cst, c, TAPS * CT)
        eps, c = carve(cst, c, 1)
        ss0, c = carve(cst, c, 3)
        r0, c = carve(cst, c, 3)
        ssd, c = carve(cst, c, NQ, DN)
        sst, c = carve(cst, c, NQ)
        rd, c = carve(cst, c, NQ)
        r2, c = carve(cst, c, SEQ)
        assert c <= 1152
        V_PRE, V_MIX, V_POST, V_FFN = 0, KT, 2 * KT, 3 * KT
        V_PS, V_BDW = 4 * KT, 4 * KT + PT
        V_LNG, V_LNB = V_BDW + CT, V_BDW + 2 * CT
        wpw, c = carve(side, 0, CT, DC)
        wpl, c = carve(side, c, NPG, PG)
        sq4, c = carve(side, c, CT, SEQ)
        acc_o, c = carve(side, c, SEQ)
        sq_o, c = carve(side, c, SEQ)
        assert c <= KT * SEQ
        GP = TAPS - 1
        SM = TOK - META + (TOK - P) + (TOK - 2 * P)
        S0, S1, S2 = 0, TOK - META, TOK - META + TOK - P
        glu, c = carve(arena, 0, CT, GP + TOK)
        xsm = arena[:, c:c + D]
        cy, c = carve(arena, c, CT, SEQ)
        mf, c = carve(arena, c, CT, SEQ)
        mask, c = carve(arena, c, SM)
        negtri, c = carve(arena, c, P)
        negones, c = carve(arena, c, P)
        rside, c = carve(arena, c, SEQ)
        ra, c = carve(arena, c, SEQ)
        qb, kb, vb, vT = [None] * 2, [None] * 2, [None] * 2, [None] * 2
        grow, e = carve(arena, c, P)
        vrow, e = carve(arena, e, P)
        drow, e = carve(arena, e, P)
        a_s, e = carve(arena, e, 2, TOK)
        sg, e = carve(arena, e, 2, TOK)
        assert e - c <= 2 * SEQ + 4 * KPAD + 3 * BLK
        qb[0], c = carve(arena, c, 2, SEQ)
        kb[0], c = carve(arena, c, 2, KPAD)
        vb[0], c = carve(arena, c, 2, KPAD)
        vT[0], c = carve(arena, c, 3, BLK)
        over = c
        qb[1], c = carve(arena, c, 2, SEQ)
        kb[1], c = carve(arena, c, 2, KPAD)
        vb[1], c = carve(arena, c, 2, KPAD)
        vT[1], c = carve(arena, c, 3, BLK)
        zm, c = carve(arena, c, 2, SM)
        lg, c = carve(arena, c, SM)
        sp, c = carve(arena, c, 2, SM)
        lw, c = carve(arena, c, 2, SM)
        wt, c = carve(arena, c, 2, SM)
        assert c <= AR
        xr, e = carve(arena, over, 3, D)
        assert e <= c
        pu, e = carve(arena, over, PT, TOK)
        pw0, e = carve(arena, e, PT, TOK)
        pw1, e = carve(arena, e, PT, TOK)
        pooled, e = carve(arena, e, PT, SEQ)
        assert e <= c
        tb, e = carve(arena, over, 2, SEQ)
        sqy, e = carve(arena, e, 2, 2, SEQ)
        accy, e = carve(arena, e, 2, SEQ)
        r1, e = carve(arena, e, SEQ)
        th, e = carve(arena, e, 2, 2, SEQ)
        assert e <= AR
        sqh, e = carve(arena, 0, KT // 2, 2 * SEQ)
        assert e <= over

        ps = ctx.enter_context(nc.psum_tensor("ps", [P, 8, 512], F32))

        def sem(name):
            return ctx.enter_context(nc.semaphore(name))

        slot_free = sem("slot_free")
        raw_landed = [sem(f"raw_landed{s}") for s in range(WSLOTS)]
        hi_done, lo_done, chunks_used = sem("hi_done"), sem("lo_done"), sem("chunks_used")
        x_landed = [sem(f"x_landed{m}") for m in range(3)]
        grow_landed, vec_landed, sw_landed, gbc_landed, stored = (
            sem("grow_landed"), sem("vec_landed"), sem("sw_landed"), sem("gbc_landed"), sem("stored"))
        const_step, const_ready, pads_ready, pads0, lg_done = (
            sem("const_step"), sem("const_ready"), sem("pads_ready"), sem("pads0"), sem("lg_done"))
        ss_dve, ss_act, r0_done, xs_dve, xs_act = (
            sem("ss_dve"), sem("ss_act"), sem("r0_done"), sem("xs_dve"), sem("xs_act"))
        grow_turned, grow_done, vec_turned, vec_done, u_made, xt_made, xt_kept, u_hi, u_lo = (
            sem("grow_turned"), sem("grow_done"), sem("vec_turned"), sem("vec_done"), sem("u_made"), sem("xt_made"),
            sem("xt_kept"), sem("u_hi"), sem("u_lo"))
        a_kept, gate_sig, glu_done, tap_done = sem("a_kept"), sem("gate_sig"), sem("glu_done"), sem("tap_done")
        pu_kept, pool_step, mix_made, pm_done, ssp_made, rp_done, pn_done, pool_hi, pool_lo = (
            sem("pu_kept"), sem("pool_step"), sem("mix_made"), sem("pm_done"), sem("ssp_made"), sem("rp_done"),
            sem("pn_done"), sem("pool_hi"), sem("pool_lo"))
        lnm_made, ln_cent, ln_sq, lnv_made, ln_r, ln_y, ln_act, pw_made, oc_done, ssc_made, rc_done, cn_done, \
            conv_hi, conv_lo = (sem(n) for n in ("lnm_made", "ln_cent", "ln_sq", "lnv_made", "ln_r", "ln_y", "ln_act",
                                                 "pw_made", "oc_done", "ssc_made", "rc_done", "cn_done",
                                                 "conv_hi", "conv_lo"))
        v_kept, q_kept, k_kept, vt_made, vt_kept = (
            sem("v_kept"), sem("q_kept"), sem("k_kept"), sem("vt_made"), sem("vt_kept"))
        z_made, zm_done, log_step, sp_done, sum_made, lw_done, wt_done, o_made, o_sq, o_hi, o_acc, o_lo = (
            sem(n) for n in ("z_made", "zm_done", "log_step", "sp_done", "sum_made", "lw_done", "wt_done", "o_made",
                             "o_sq", "o_hi", "o_acc", "o_lo"))
        ssa_made, ra_done, t_done, y_done, y_sq, y_gain, y_acc = (
            sem(n) for n in ("ssa_made", "ra_done", "t_done", "y_done", "y_sq", "y_gain", "y_acc"))
        ssy_made, r1_done, th_done, h2_done, h2_hi, h2_lo, h2_sq, h2_acc, ss2_made, r2_done, rows_made, rows_kept = (
            sem(n) for n in ("ssy_made", "r1_done", "th_done", "h2_done", "h2_hi", "h2_lo", "h2_sq", "h2_acc",
                             "ss2_made", "r2_done", "rows_made", "rows_kept"))
        gs_done, silu_done, us_done, p_done, f_hi, f_lo = (
            sem(n) for n in ("gs_done", "silu_done", "us_done", "p_done", "f_hi", "f_lo"))
        down_free, dsq_done, f_done, sst_done, rd_done, res_done = (
            sem(n) for n in ("down_free", "dsq_done", "f_done", "sst_done", "rd_done", "res_done"))

        def tiles(w):
            return w.rearrange("a (kt p) n -> p (a kt) n", p=P)

        win_v, wout_v, wg_v, wu_v, wd_v = tiles(w_in), tiles(w_out), tiles(w_gate), tiles(w_up), tiles(w_down)
        out_v = out.rearrange("a (m p) d -> p (a m) d", p=P)

        block = ctx.enter_context(nc.Block())

        @block.sync
        def _(sp_eng):
            sp_eng.dma_start(xr[0:META, 2, :], meta).then_inc(x_landed[2], 16)
            for m in range(NQ):
                sp_eng.dma_start(xr[:, m, :], x[0, m * P:(m + 1) * P, :]).then_inc(x_landed[m], 16)
            sp_eng.dma_start(grow[0:KT, :], pre_mix_g.rearrange("a (c p) -> (a c) p", p=P)).then_inc(grow_landed, 16)

            def load(src, kt, n0, q, slot, kts=CK, cols=BLK, wait=True):
                if wait:
                    sp_eng.wait_ge(lo_done, q - WSLOTS + 1)
                    if not isinstance(q, int):
                        sp_eng.sem_inc(slot_free, 1)
                sp_eng.dma_start(raw[:, slot, :].rearrange("p (k n) -> p k n", k=kts),
                                 src[:, kt:kt + kts, bass.ds(n0, cols)]).then_inc(raw_landed[slot], 16)

            for i in range(2):
                for b, col in enumerate((C_A, C_GATE)):
                    for s in range(CK):
                        q = Q_CONV + (2 * i + b) * CK + s
                        load(win_v, s * CK, col + i * BLK, q, s, wait=q >= WSLOTS)
            with sp_eng.Fori(0, 2) as i:
                for s in range(CK):
                    load(win_v, s * CK, C_POOL + i * BLK, i * CK + (Q_POOL + s), s)
            with sp_eng.Fori(0, GROUPS) as g:
                for b, col in enumerate((2 * DA, 0, DA)):
                    for s in range(CK):
                        load(win_v, s * CK, col + g * BLK, g * PER_G + (Q_ATT + b * CK + s), s)
            for n, (part, j) in enumerate(out_parts):
                for s in range(OC):
                    q = Q_OUT + n * OC + s
                    kt = (DA // P if part == "side" else 0) + s * CK
                    load(wout_v, kt, j * BLK, q, q % WSLOTS)
            with sp_eng.Fori(0, NFB) as i:
                for b, src in enumerate((wg_v, wu_v)):
                    for s in range(CK):
                        load(src, s * CK, i * BLK, i * 2 * CK + (Q_FFN + b * CK + s), s)
            with sp_eng.Fori(0, DN // 2) as i:
                for b in range(2):
                    for d in range(DCH):
                        load(wd_v, 2 * d, i * 2 * DCOLS + b * DCOLS, i * 2 * DCH + (Q_DOWN + b * DCH + d),
                             (b * DCH + d) % WSLOTS, kts=2, cols=DCOLS)
            for m in range(NQ):
                for n in range(2):
                    half = slice(n * D // 2, (n + 1) * D // 2)
                    sp_eng.wait_ge(res_done, 2 * m + n + 1)
                    sp_eng.dma_start(out_v[:, m, half], f_acc[:, m, half]).then_inc(stored, 16)
            sp_eng.wait_ge(stored, 16 * 2 * NQ)

        @block.gpsimd
        def _(pool):
            pool.memset(ident, 0.0).then_inc(const_step, 1)
            pool.memset(ones, 1.0).then_inc(const_step, 1)
            pool.memset(eps, EPS).then_inc(const_step, 1)
            pool.memset(negtri, -1.0).then_inc(const_step, 1)
            pool.memset(negones, -1.0).then_inc(const_step, 1)
            pool.memset(mask, 0.0).then_inc(const_step, 1)
            pool.wait_ge(const_step, 6)
            pool.affine_select(ident, ident, [[-1, P]], ALU.not_equal, 1.0, base=0,
                               channel_multiplier=1).then_inc(const_ready, 1)
            pool.affine_select(negtri, negtri, [[-1, P]], ALU.is_ge, 0.0, base=0,
                               channel_multiplier=1).then_inc(const_ready, 1)
            for at, n, base in ((S0, P - META, META), (S1, P, 0), (S2, TOK - 2 * P, 0)):
                pool.affine_select(mask[:, at:at + n], mask[:, at:at + n], [[1, n]], ALU.is_gt, NEG, base=base,
                                   channel_multiplier=-1).then_inc(const_ready, 1)
            at = 0
            for v in (mix_out_g, post_mix_g, pre_ffn_g, pool_scale, b_dw, conv_ln_g, conv_ln_b):
                n = v.shape[1] // P
                pool.dma_start(vrow[at:at + n, :], v.rearrange("a (c p) -> (a c) p", p=P)).then_inc(vec_landed, 16)
                at += n
            pool.dma_start(drow[0:TAPS * CT, :], w_dw.rearrange("a w (c p) -> (a w c) p", p=P)).then_inc(vec_landed, 16)
            pool.dma_start(wpl, w_pool.rearrange("a g c d -> c (a g) d")).then_inc(sw_landed, 16)
            pool.dma_start(wpw, w_pw.rearrange("a (c p) n -> p (a c) n", p=P)).then_inc(sw_landed, 16)
            pool.memset(glu[:, :, 0:GP], 0.0).then_inc(pads_ready, 1)
            pool.wait_ge(glu_done, 2)
            pool.memset(kb[0][:, :, TOK:KPAD], 0.0).then_inc(pads0, 1)
            pool.memset(vb[0][:, :, TOK:KPAD], 0.0).then_inc(pads0, 1)
            pool.wait_ge(pn_done, PT)
            pool.memset(kb[1][:, :, TOK:KPAD], 0.0).then_inc(pads_ready, 1)
            pool.memset(vb[1][:, :, TOK:KPAD], 0.0).then_inc(pads_ready, 1)

        def hi_view(ap):
            return ap.bitcast(F32)

        @block.scalar
        def _(act):
            def split_hi(q, slot, turn):
                act.wait_ge(raw_landed[slot], 16 * (turn + 1))
                if not isinstance(q, int) or q >= WSLOTS:
                    act.wait_ge(chunks_used, q - WSLOTS + 1)
                act.activation(w_hi[:, slot, :], raw[:, slot, :], ACT.Copy).then_inc(hi_done, 1)

            def split(q):
                split_hi(q, q % WSLOTS, q // WSLOTS)

            step = [0]

            def inv_rms(dst, src, n, done):
                act.activation(dst, src, ACT.Ln, bias=eps[0:dst.shape[0]], scale=1.0 / n).then_inc(log_step, 1)
                step[0] += 1
                act.wait_ge(log_step, step[0])
                act.activation(dst, dst, ACT.Exp, scale=-0.5).then_inc(done, 1)

            act.preload_act_table_set("natural_log_exp_and_others")
            act.wait_ge(const_step, 6)
            act.wait_ge(x_landed[2], 16)
            act.activation(xsm[0:META], xr[0:META, 2, :], ACT.Square, accum_out=ss0[0:META, 2:3]).then_inc(ss_act, 1)
            act.wait_ge(ss_act, 1)
            inv_rms(r0[0:META, 2:3], ss0[0:META, 2:3], D, r0_done)
            act.wait_ge(x_landed[1], 16)
            act.activation(xs[:, 1, :], xr[:, 1, :], ACT.Square, accum_out=ss0[:, 1:2]).then_inc(ss_act, 1)
            act.wait_ge(ss_act, 2)
            act.wait_ge(ss_dve, 1)
            inv_rms(r0[:, 0:2], ss0[:, 0:2], D, r0_done)
            act.wait_ge(r0_done, 2)
            act.activation(xs[:, 1, 0:D // 2], xr[:, 1, 0:D // 2], ACT.Copy, scale=r0[:, 1:2]).then_inc(xs_act, 1)
            act.wait_ge(grow_turned, 1)
            act.copy(vec[:, 0:KT], ps[:, 0, 0:KT]).then_inc(grow_done, 1)
            act.wait_ge(grow_done, 1)
            for kt in range(KT):
                act.wait_ge(u_made, kt + 1)
                act.activation(u[:, kt, 0, :], ps[:, 4 + kt % 4, 0:TOK], ACT.Copy,
                               scale=vec[:, V_PRE + kt:V_PRE + kt + 1]).then_inc(u_hi, 1)
                if kt % CK == CK - 1:
                    split(kt // CK)

            def soft(n):
                act.wait_ge(zm_done, n + 1)
                if n >= 1:
                    act.wait_ge(sp_done, n)
                act.activation(lg, zm[:, n % 2], ACT.Abs).then_inc(log_step, 1)
                step[0] += 1
                act.wait_ge(log_step, step[0])
                act.activation(lg, lg, ACT.Exp, scale=-1.0).then_inc(log_step, 1)
                step[0] += 1
                act.wait_ge(log_step, step[0])
                act.activation(lg, lg, ACT.Ln, bias=1.0).then_inc(lg_done, 1)

            def weights(n):
                act.wait_ge(lw_done, n + 1)
                if n >= 2:
                    act.wait_ge(o_made, n - 1)
                act.activation(wt[:, n % 2], lw[:, n % 2], ACT.Exp).then_inc(wt_done, 1)

            def head_pair_out(n):
                kt = n // 2
                o = ps[:, 7, (kt % 2) * SEQ:(kt % 2 + 1) * SEQ]
                act.wait_ge(o_made, n + 1)
                if kt >= 1:
                    act.wait_ge(o_acc, kt)
                act.activation(sq_o, o, ACT.Square).then_inc(o_sq, 1)
                act.activation(ffn[:, kt, 0, :], o, ACT.Copy, scale=vec[:, V_MIX + kt:V_MIX + kt + 1]).then_inc(o_hi, 1)

            def y_squares(j):
                act.wait_ge(y_done, j + 1)
                if j >= 2:
                    act.wait_ge(y_acc, j - 1)
                act.activation(sqy[:, j % 2], y[:, 2 * j:2 * j + 2, :], ACT.Square).then_inc(y_sq, 1)
                act.wait_ge(y_sq, j + 1)
                for kt in (2 * j, 2 * j + 1):
                    act.activation(y[:, kt, :], y[:, kt, :], ACT.Copy,
                                   scale=vec[:, V_POST + kt:V_POST + kt + 1]).then_inc(y_gain, 1)

            for q in range(WSLOTS, Q_FFN + CK):
                split(q)
                e = q - 4
                if q == VEC_AT + LAG:
                    act.wait_ge(vec_turned, 1)
                    act.copy(vec[:, KT:NV], ps[:, 7, 0:NB]).then_inc(vec_done, 1)
                    act.copy(dw, ps[:, 7, P:P + TAPS * CT]).then_inc(vec_done, 1)
                if 0 <= q - LAG - TURN_AT < NOB:
                    j = q - LAG - TURN_AT
                    act.wait_ge(xt_made, j + 1)
                    if j == 0:
                        act.wait_ge(u_made, KT)
                    act.copy(xT[:, 2 * j:2 * j + 2, :],
                             ps[:, 4 + j % 4, :].rearrange("p (a t) -> p a t", a=2)).then_inc(xt_kept, 1)
                for i in range(2):
                    if e == Q_CONV + 2 * i * CK + CK - 1:
                        act.wait_ge(chunks_used, e + 1)
                        if i:
                            act.wait_ge(glu_done, 1)
                        act.copy(a_s, ps[:, 0:2, 0:TOK]).then_inc(a_kept, 1)
                    if e == Q_CONV + 2 * i * CK + 2 * CK - 1:
                        act.wait_ge(chunks_used, e + 1)
                        act.activation(sg, ps[:, 2:4, 0:TOK], ACT.Sigmoid).then_inc(gate_sig, 1)
                        act.preload_act_table_set("natural_log_exp_and_others")
                    if e == Q_POOL + (i + 1) * CK - 1:
                        act.wait_ge(chunks_used, e + 1)
                        if i == 0:
                            act.wait_ge(xt_made, NOB)
                        b = pool_bank[i]
                        act.copy(pu[:, 2 * i:2 * i + 2, :], ps[:, b:b + 2, 0:TOK]).then_inc(pu_kept, 1)
                if Q_ATT <= e < Q_OUT:
                    g, b = (e - Q_ATT) // PER_G, (e - Q_ATT) % PER_G
                    if b % CK == CK - 1:
                        act.wait_ge(chunks_used, e + 1)
                        if b < CK:
                            if g == 1:
                                act.wait_ge(pads_ready, 3)
                            if g >= 2:
                                act.wait_ge(vt_made, g - 1)
                            act.copy(vb[g % 2][:, :, 0:TOK], ps[:, 2:4, 0:TOK]).then_inc(v_kept, 1)
                        elif b < 2 * CK:
                            if g >= 2:
                                act.wait_ge(z_made, HPG * (g - 1))
                            act.mul(qb[g % 2], ps[:, 4, :].rearrange("p (m t) -> p m t", m=2),
                                    DH ** -0.5).then_inc(q_kept, 1)
                        else:
                            if g >= 2:
                                act.wait_ge(z_made, HPG * (g - 1))
                            act.copy(kb[g % 2][:, :, 0:TOK], ps[:, 0:2, 0:TOK]).then_inc(k_kept, 1)
                if q - LAG in VT_AT:
                    g = VT_AT[q - LAG]
                    act.wait_ge(vt_made, g + 1)
                    if g >= 2:
                        act.wait_ge(o_made, HPG * (g - 1))
                    for m in range(2):
                        act.copy(vT[g % 2][:, :, m * P:(m + 1) * P],
                                 ps[:, 5 + m, 0:KPAD].rearrange("p (k d) -> p k d", k=3)).then_inc(vt_kept, 1)
                if q - 5 in HEAD_AT:
                    weights(HEAD_AT[q - 5])
                if q - 3 in HEAD_AT:
                    soft(HEAD_AT[q - 3])
                if q - 7 in HEAD_AT and HEAD_AT[q - 7] % 2:
                    head_pair_out(HEAD_AT[q - 7])

                if q == PE_MIX + LAG:
                    act.wait_ge(mix_made, 1)
                    for g in range(NPG):
                        act.activation(mf[:, g, :], ps[:, 5 + g // 2, (g % 2) * SEQ:(g % 2 + 1) * SEQ], ACT.Copy,
                                       scale=vec[:, V_PS + g:V_PS + g + 1]).then_inc(pm_done, 1)
                    act.wait_ge(pm_done, NPG)
                    act.activation(sq4, mf, ACT.Square).then_inc(pm_done, 1)
                if q == PE_SSP + LAG:
                    act.wait_ge(ssp_made, 1)
                    inv_rms(rside, ps[:, 7, 0:SEQ], DP, rp_done)
                if q == PE_SSP + LAG + 1:
                    act.wait_ge(pn_done, PT)
                    act.copy(ffn[:, DA // P:DA // P + PT, 0, :], mf).then_inc(pool_hi, 1)

                if q == PE_LNM + LAG + 1:
                    act.wait_ge(ln_cent, CT)
                    act.activation(sq4, cy, ACT.Square).then_inc(ln_sq, 1)
                if q == PE_LNV + LAG:
                    act.wait_ge(lnv_made, 1)
                    act.wait_ge(pn_done, PT)
                    inv_rms(rside, ps[:, 0, 0:SEQ], DC, ln_r)
                if q == PE_LNV + LAG + 2:
                    act.wait_ge(ln_y, CT)
                    act.wait_ge(pool_lo, 1)
                    for t in range(CT):
                        act.activation(mf[:, t, :], cy[:, t, :], ACT.Silu,
                                       bias=vec[:, V_LNB + t:V_LNB + t + 1]).then_inc(ln_act, 1)
                    act.preload_act_table_set("natural_log_exp_and_others")
                if q == PE_PW + LAG + 1:
                    act.wait_ge(pw_made, 2)
                    act.copy(cy, ps[:, 0:2, :].rearrange("p b (c t) -> p (b c) t", c=2)).then_inc(oc_done, 1)
                    act.activation(sq4, ps[:, 0:2, :].rearrange("p b (c t) -> p (b c) t", c=2),
                                   ACT.Square).then_inc(oc_done, 1)
                if q == PE_SSC + LAG:
                    act.wait_ge(ssc_made, 1)
                    inv_rms(rside, ps[:, 2, 0:SEQ], DC, rc_done)
                if q == PE_SSC + LAG + 1:
                    act.wait_ge(cn_done, CT)
                    act.copy(ffn[:, (DA + DP) // P:KT, 0, :], mf).then_inc(conv_hi, 1)

                if q == PE_SSA + LAG:
                    act.wait_ge(ssa_made, 1)
                    inv_rms(ra, ps[:, 7, 0:SEQ], DA, ra_done)
                if q - 1 in OUT_EVAC:
                    y_squares(OUT_EVAC[q - 1])

            y_squares(NOB - 1)
            act.wait_ge(ssy_made, 1)
            inv_rms(r1, ps[:, 1, 0:SEQ], D, r1_done)
            for j in range(NOB):
                act.wait_ge(h2_done, j + 1)
                for kt in (2 * j, 2 * j + 1):
                    act.activation(u[:, kt, 0, 0:SEQ], xT[:, kt, :], ACT.Copy,
                                   scale=vec[:, V_FFN + kt:V_FFN + kt + 1]).then_inc(h2_hi, 1)
                act.activation(sqh[:, j, :], xT[:, 2 * j:2 * j + 2, :].rearrange("p a t -> p (a t)"),
                               ACT.Square).then_inc(h2_sq, 1)
                if j in (5, 7):
                    split(Q_FFN + CK + (j - 5) // 2)
            split(Q_FFN + CK + 2)
            split(Q_FFN + CK + 3)
            act.wait_ge(ss2_made, 1)
            inv_rms(r2, ps[:, 7, 0:SEQ], D, r2_done)
            for n in range(2 * DN):
                act.wait_ge(rows_made, n + 1)
                act.copy(h2rows[:, n // DN, (n % DN) * DCOLS:(n % DN + 1) * DCOLS],
                         ps[:, 2 + n % 4, :]).then_inc(rows_kept, 1)
            act.wait_ge(rows_kept, 2 * DN)
            act.sem_inc(down_free, 4)
            act.dma_start(gbc[:, :], post_ffn_g.to_broadcast([P, D])).then_inc(gbc_landed, 16)

            def silu(i):
                act.wait_ge(gs_done, i + 1)
                act.activation(tmp_ffn[:, 1, :], tmp_ffn[:, 0, :], ACT.Silu).then_inc(silu_done, 1)

            silu0 = Q_FFN + 2 * CK
            with act.Fori(0, NFB - 1) as i:
                silu(i)
                for s in range(2 * CK):
                    split_hi(i * 2 * CK + (silu0 + s), s % WSLOTS, i * 2 + (silu0 + s) // WSLOTS)
            silu(NFB - 1)

            for q in range(Q_DOWN, Q_DOWN + DN * DCH + 4):
                if q < Q_DOWN + DN * DCH:
                    split(q)
                if q == Q_DOWN + 4:
                    act.preload_act_table_set("natural_log_exp_and_others")
                n, rest = (q - 4 - Q_DOWN) // DCH, (q - 4 - Q_DOWN) % DCH
                if q - 4 >= Q_DOWN and rest == DCH - 1:
                    act.wait_ge(chunks_used, q - 3)
                    for m in range(NQ):
                        if n or m:
                            act.wait_ge(dsq_done, NQ * n + m)
                        if m:
                            act.wait_ge(f_done, NQ * n + 1)
                        act.activation(tmp_ffn[:, 0, :], ps[:, 2 + 2 * (n % 2) + m, :], ACT.Square,
                                       accum_out=ssd[:, m, n:n + 1]).then_inc(dsq_done, 1)
                    act.wait_ge(dsq_done, NQ * (n + 1))
                    act.sem_inc(down_free, 1)
            act.wait_ge(sst_done, 1)
            inv_rms(rd, sst, D, rd_done)

        @block.vector
        def _(dve):
            def split_lo(q, slot):
                dve.wait_ge(hi_done, q + 1)
                dve.tensor_tensor(w_lo[:, slot, :], raw[:, slot, :], hi_view(w_hi[:, slot, :]),
                                  ALU.subtract).then_inc(lo_done, 1)

            def split(q):
                split_lo(q, q % WSLOTS)

            dve.wait_ge(x_landed[0], 16)
            dve.scalar_tensor_tensor(xs[:, 0, :], xr[:, 0, :], 1.0, xr[:, 0, :], ALU.mult, ALU.mult,
                                     accum_out=ss0[:, 0:1]).then_inc(ss_dve, 1)
            dve.wait_ge(r0_done, 1)
            dve.tensor_scalar(xsm[0:META], xr[0:META, 2, :], r0[0:META, 2:3], None, ALU.mult).then_inc(xs_dve, 1)
            dve.wait_ge(r0_done, 2)
            dve.wait_ge(ss_dve, 1)
            for m, n in ((0, 0), (0, 1), (1, 1)):
                half = slice(n * D // 2, (n + 1) * D // 2)
                dve.tensor_scalar(xs[:, m, half], xr[:, m, half], r0[:, m:m + 1], None, ALU.mult).then_inc(xs_dve, 1)
            for kt in range(KT):
                dve.wait_ge(u_hi, kt + 1)
                dve.scalar_tensor_tensor(u[:, kt, 1, :], ps[:, 4 + kt % 4, 0:TOK], vec[:, V_PRE + kt:V_PRE + kt + 1],
                                         hi_view(u[:, kt, 0, :]), ALU.mult, ALU.subtract).then_inc(u_lo, 1)
                if kt % CK == CK - 1:
                    split(kt // CK)

            def masked(n):
                dve.wait_ge(z_made, n + 1)
                dve.tensor_tensor(zm[:, n % 2], ps[:, 5 + n % 2, 0:SM], mask, ALU.add).then_inc(zm_done, 1)

            def softplus(n):
                dve.wait_ge(lg_done, n + 1)
                dve.scalar_tensor_tensor(sp[:, n % 2], zm[:, n % 2], 0.0, lg, ALU.max, ALU.add).then_inc(sp_done, 1)

            def log_weights(n):
                dve.wait_ge(sum_made, n + 1)
                if n >= 2:
                    dve.wait_ge(wt_done, n - 1)
                dve.scalar_tensor_tensor(lw[:, n % 2], ps[:, 5 + n % 2, 0:SM], 0.0, mask,
                                         ALU.min, ALU.add).then_inc(lw_done, 1)

            def head_pair_out(n):
                kt = n // 2
                dve.wait_ge(o_hi, kt + 1)
                dve.scalar_tensor_tensor(ffn[:, kt, 1, :], ps[:, 7, (kt % 2) * SEQ:(kt % 2 + 1) * SEQ],
                                         vec[:, V_MIX + kt:V_MIX + kt + 1], hi_view(ffn[:, kt, 0, :]),
                                         ALU.mult, ALU.subtract).then_inc(o_lo, 1)
                dve.wait_ge(o_sq, kt + 1)
                if kt == 0:
                    dve.tensor_copy(acc_o, sq_o).then_inc(o_acc, 1)
                else:
                    dve.wait_ge(o_acc, kt)
                    dve.tensor_tensor(acc_o, acc_o, sq_o, ALU.add).then_inc(o_acc, 1)

            def both(r):
                return r.rearrange("p (a t) -> p a t", a=1).to_broadcast([P, 2, SEQ])

            def add_squares(j):
                dve.wait_ge(y_sq, j + 1)
                if j == 0:
                    dve.tensor_copy(accy, sqy[:, 0]).then_inc(y_acc, 1)
                else:
                    dve.wait_ge(y_acc, j)
                    dve.tensor_tensor(accy, accy, sqy[:, j % 2], ALU.add).then_inc(y_acc, 1)

            def input_lo(j):
                for kt in (2 * j, 2 * j + 1):
                    dve.wait_ge(h2_hi, kt + 1)
                    dve.scalar_tensor_tensor(u[:, kt, 1, 0:SEQ], xT[:, kt, :], vec[:, V_FFN + kt:V_FFN + kt + 1],
                                             hi_view(u[:, kt, 0, 0:SEQ]), ALU.mult, ALU.subtract).then_inc(h2_lo, 1)

            for q in range(WSLOTS, Q_FFN + CK):
                split(q)
                if q - 5 in HEAD_AT:
                    log_weights(HEAD_AT[q - 5])
                if q - 3 in HEAD_AT:
                    masked(HEAD_AT[q - 3])
                if q - 7 in HEAD_AT and HEAD_AT[q - 7] % 2:
                    head_pair_out(HEAD_AT[q - 7])
                for i in range(2):
                    if q - 4 == Q_CONV + 2 * i * CK + 2 * CK - 1:
                        dve.wait_ge(a_kept, i + 1)
                        dve.wait_ge(gate_sig, i + 1)
                        dve.tensor_tensor(glu[:, 2 * i:2 * i + 2, GP:GP + TOK], a_s, sg, ALU.mult).then_inc(glu_done, 1)
                w = q - Q_TAPS
                if 0 <= w < TAPS:
                    if w == 0:
                        dve.wait_ge(vec_done, 2)
                        dve.wait_ge(pads_ready, 1)
                        dve.wait_ge(glu_done, 2)
                    for t in range(CT):
                        src = glu[:, t, META + w:META + w + SEQ]
                        tap = dw[:, w * CT + t:w * CT + t + 1]
                        if w == 0:
                            dve.tensor_scalar(cy[:, t, :], src, tap, vec[:, V_BDW + t:V_BDW + t + 1],
                                              ALU.mult, ALU.add).then_inc(tap_done, 1)
                        else:
                            dve.wait_ge(tap_done, (w - 1) * CT + t + 1)
                            dve.scalar_tensor_tensor(cy[:, t, :], src, tap, cy[:, t, :],
                                                     ALU.mult, ALU.add).then_inc(tap_done, 1)
                if q - 3 in HEAD_AT:
                    softplus(HEAD_AT[q - 3])
                if q == Q_POOL + 2 * CK + LAG + 1:
                    dve.wait_ge(pu_kept, 2)
                    src = pu
                    for n in range(NPG):
                        d = 1 << n
                        lo = 2 * d - 1
                        dst = (pw0, pw1)[n % 2]
                        dve.tensor_tensor(dst[:, n:NPG, lo:TOK], src[:, n:NPG, lo:TOK], src[:, n:NPG, lo - d:TOK - d],
                                          ALU.add).then_inc(pool_step, 1)
                        dve.wait_ge(pool_step, 2 * n + 1)
                        dve.scalar_tensor_tensor(pooled[:, n, :], dst[:, n, META:TOK], 1.0 / (2 * d), pu[:, n, META:TOK],
                                                 ALU.mult, ALU.subtract).then_inc(pool_step, 1)
                        src = dst
                if q == PE_SSP + LAG:
                    dve.wait_ge(rp_done, 1)
                    for t in range(PT):
                        g = V_MIX + DA // P + t
                        dve.scalar_tensor_tensor(mf[:, t, :], mf[:, t, :], vec[:, g:g + 1], rside,
                                                 ALU.mult, ALU.mult).then_inc(pn_done, 1)
                if q == PE_SSP + LAG + 1:
                    dve.wait_ge(pool_hi, 1)
                    at = DA // P
                    dve.tensor_tensor(ffn[:, at:at + PT, 1, :], mf, hi_view(ffn[:, at:at + PT, 0, :]),
                                      ALU.subtract).then_inc(pool_lo, 1)
                if q == PE_LNM + LAG:
                    dve.wait_ge(lnm_made, 1)
                    for t in range(CT):
                        dve.scalar_tensor_tensor(cy[:, t, :], ps[:, 0, 0:SEQ], -1.0 / DC, cy[:, t, :],
                                                 ALU.mult, ALU.add).then_inc(ln_cent, 1)
                if q == PE_LNV + LAG + 1:
                    dve.wait_ge(ln_r, 1)
                    for t in range(CT):
                        dve.scalar_tensor_tensor(cy[:, t, :], cy[:, t, :], vec[:, V_LNG + t:V_LNG + t + 1], rside,
                                                 ALU.mult, ALU.mult).then_inc(ln_y, 1)
                if q == PE_SSC + LAG:
                    dve.wait_ge(rc_done, 1)
                    for t in range(CT):
                        g = V_MIX + (DA + DP) // P + t
                        dve.scalar_tensor_tensor(mf[:, t, :], cy[:, t, :], vec[:, g:g + 1], rside,
                                                 ALU.mult, ALU.mult).then_inc(cn_done, 1)
                if q == PE_SSC + LAG + 1:
                    dve.wait_ge(conv_hi, 1)
                    at = (DA + DP) // P
                    dve.tensor_tensor(ffn[:, at:KT, 1, :], mf, hi_view(ffn[:, at:KT, 0, :]),
                                      ALU.subtract).then_inc(conv_lo, 1)
                if q in OUT_EVAC:
                    j = OUT_EVAC[q]
                    dve.wait_ge(chunks_used, q - 3)
                    dve.wait_ge(ra_done, 1)
                    dve.tensor_tensor(tb, ps[:, attn_bank[j], :].rearrange("p (m t) -> p m t", m=2), both(ra),
                                      ALU.mult).then_inc(t_done, 1)
                    dve.wait_ge(t_done, j + 1)
                    dve.tensor_tensor(y[:, 2 * j:2 * j + 2, :], tb,
                                      ps[:, side_bank[j], :].rearrange("p (m t) -> p m t", m=2),
                                      ALU.add).then_inc(y_done, 1)
                    if j:
                        add_squares(j - 1)

            dve.wait_ge(r1_done, 1)
            for j in range(NOB + 1):
                if j < NOB:
                    dve.wait_ge(y_gain, 2 * j + 2)
                    if j >= 2:
                        dve.wait_ge(h2_done, j - 1)
                    dve.tensor_tensor(th[:, j % 2], y[:, 2 * j:2 * j + 2, :], both(r1), ALU.mult).then_inc(th_done, 1)
                if j == 0:
                    continue
                if j >= 2:
                    input_lo(j - 2)
                pair = slice(2 * j - 2, 2 * j)
                dve.wait_ge(th_done, j)
                dve.tensor_tensor(xT[:, pair, :], th[:, (j - 1) % 2], xT[:, pair, :], ALU.add).then_inc(h2_done, 1)
                if j in (6, 8):
                    split(Q_FFN + CK + (j - 6) // 2)
            input_lo(NOB - 1)
            split(Q_FFN + CK + 2)
            acc2 = accy.rearrange("p a t -> p (a t)")
            for j in range(1, NOB):
                dve.wait_ge(h2_sq, j + 1)
                if j >= 2:
                    dve.wait_ge(h2_acc, j - 1)
                dve.tensor_tensor(acc2, sqh[:, 0, :] if j == 1 else acc2, sqh[:, j, :], ALU.add).then_inc(h2_acc, 1)
            split(Q_FFN + 2 * CK - 1)

            def halves(ap):
                return ap.rearrange("p (a t) -> p a t", a=2)

            def gate_evac(i):
                dve.wait_ge(chunks_used, i * 2 * CK + (Q_FFN + CK))
                dve.tensor_tensor(halves(tmp_ffn[:, 0, :]), halves(ps[:, 0, :]), both(r2), ALU.mult).then_inc(gs_done, 1)

            def up_evac(i):
                dve.wait_ge(chunks_used, i * 2 * CK + (Q_FFN + 2 * CK))
                dve.tensor_tensor(halves(tmp_ffn[:, 2, :]), halves(ps[:, 1, :]), both(r2), ALU.mult).then_inc(us_done, 1)
                dve.wait_ge(silu_done, i + 1)
                dve.wait_ge(us_done, i + 1)
                dve.tensor_tensor(tmp_ffn[:, 3, :], tmp_ffn[:, 1, :], tmp_ffn[:, 2, :], ALU.mult).then_inc(p_done, 1)
                sl, us, p = (tmp_ffn[:, n, :].rearrange("p (a t) -> p a t", a=2) for n in (1, 2, 3))
                dve.tensor_tensor(ffn[:, bass.ds(2 * i, 2), 0, :], sl, us, ALU.mult).then_inc(f_hi, 1)
                dve.wait_ge(f_hi, i + 1)
                dve.wait_ge(p_done, i + 1)
                dve.tensor_tensor(ffn[:, bass.ds(2 * i, 2), 1, :], p, hi_view(ffn[:, bass.ds(2 * i, 2), 0, :]),
                                  ALU.subtract).then_inc(f_lo, 1)

            dve.wait_ge(r2_done, 1)
            dve.wait_ge(rows_made, 2 * DN)
            with dve.Fori(0, NFB - 1) as i:
                gate_evac(i)
                for s in range(CK):
                    split_lo(i * 2 * CK + (Q_FFN + 2 * CK + s), s)
                up_evac(i)
                for s in range(CK):
                    split_lo(i * 2 * CK + (Q_FFN + 3 * CK + s), s)
            gate_evac(NFB - 1)
            for q in range(Q_DOWN, Q_DOWN + DN * DCH + 4):
                if q < Q_DOWN + DN * DCH:
                    split(q)
                if q == Q_DOWN + 3:
                    up_evac(NFB - 1)
                n, rest = (q - 4 - Q_DOWN) // DCH, (q - 4 - Q_DOWN) % DCH
                if q - 4 >= Q_DOWN and rest == DCH - 1:
                    cols = slice(n * DCOLS, (n + 1) * DCOLS)
                    dve.wait_ge(chunks_used, q - 3)
                    if n == 0:
                        dve.wait_ge(gbc_landed, 16)
                    for m in reversed(range(NQ)):
                        if m == 0:
                            dve.wait_ge(dsq_done, NQ * n + 1)
                        dve.tensor_tensor(f_acc[:, m, cols], ps[:, 2 + 2 * (n % 2) + m, :], gbc[:, cols],
                                          ALU.mult).then_inc(f_done, 1)
                    dve.wait_ge(f_done, NQ * (n + 1))
                    dve.sem_inc(down_free, 1)
            dve.wait_ge(dsq_done, NQ * DN)
            dve.tensor_reduce(sst, ssd, AX.X, ALU.add).then_inc(sst_done, 1)
            dve.wait_ge(rd_done, 1)
            for m in range(NQ):
                for n in range(2):
                    half = slice(n * D // 2, (n + 1) * D // 2)
                    dve.scalar_tensor_tensor(f_acc[:, m, half], f_acc[:, m, half], rd[:, m:m + 1],
                                             h2rows[:, m, half], ALU.mult, ALU.add).then_inc(res_done, 1)

        @block.tensor
        def _(pe):
            def products(q, slot, kts, rhs, outs, first, last, one_bank):
                pe.wait_ge(lo_done, q + 1)
                for k, kt in enumerate(kts):
                    x_hi, x_lo = rhs(kt)
                    for m in range(2):
                        at = slice(k * BLK + m * P, k * BLK + (m + 1) * P)
                        start = first and k == 0
                        pe.matmul(outs[m], w_hi[:, slot, at], x_hi, start=start and not (one_bank and m), stop=False,
                                  skip_group_check=True)
                        pe.matmul(outs[m], w_hi[:, slot, at], x_lo, start=False, stop=False, skip_group_check=True)
                        mm = pe.matmul(outs[m], w_lo[:, slot, at], x_hi, start=False,
                                       stop=last and k == len(kts) - 1, skip_group_check=True)
                mm.then_inc(chunks_used, 1)

            def normed(kt, lo=0):
                return u[:, kt, 0, lo:TOK], u[:, kt, 1, lo:TOK]

            def ffn_input(kt):
                return u[:, kt, 0, 0:SEQ], u[:, kt, 1, 0:SEQ]

            def merged(kt):
                return ffn[:, kt, 0, :], ffn[:, kt, 1, :]

            def two(bank):
                return [ps[:, bank, 0:SEQ], ps[:, bank, SEQ:2 * SEQ]]

            def wide(bank):
                return [ps[:, bank, 0:TOK], ps[:, bank + 1, 0:TOK]]

            def column_sums(dst, srcs, made):
                for n, s in enumerate(srcs):
                    mm = pe.matmul(dst, ones, s, start=n == 0, stop=n == len(srcs) - 1)
                mm.then_inc(made, 1)

            pe.wait_ge(const_ready, 1)
            pe.wait_ge(grow_landed, 16)
            pe.transpose(ps[:, 0, 0:KT], grow[0:KT, :], ident[0:KT, 0:KT]).then_inc(grow_turned, 1)
            for kt in range(KT):
                if kt in (0, KT // 2):
                    pe.wait_ge(xs_dve, 2 if kt == 0 else 4)
                if kt == 0:
                    pe.wait_ge(xs_act, 1)
                if kt >= 4:
                    pe.wait_ge(u_lo, kt - 3)
                b, cols = 4 + kt % 4, slice(kt * P, (kt + 1) * P)
                pe.transpose(ps[:, b, 0:META], xsm[0:META, cols], ident[0:META, 0:META])
                pe.transpose(ps[:, b, META:META + P], xs[:, 0, cols], ident)
                pe.transpose(ps[:, b, META + P:TOK], xs[:, 1, cols], ident).then_inc(u_made, 1)

            def early_work(q):
                if q == VEC_AT:
                    pe.wait_ge(u_lo, KT)
                    pe.wait_ge(vec_landed, 16 * 8)
                    pe.transpose(ps[:, 7, 0:NB], vrow[0:NB, :], ident[0:NB, 0:NB])
                    pe.transpose(ps[:, 7, P:P + TAPS * CT], drow[0:TAPS * CT, :],
                                 ident[0:TAPS * CT, 0:TAPS * CT]).then_inc(vec_turned, 1)
                if 0 <= q - TURN_AT < NOB:
                    j = q - TURN_AT
                    if j == 3:
                        pe.wait_ge(vec_done, 2)
                    if j >= 4:
                        pe.wait_ge(xt_kept, j - 3)
                    for kt in (2 * j, 2 * j + 1):
                        for m in range(NQ):
                            at = (kt % 2 * NQ + m) * P
                            mm = pe.transpose(ps[:, 4 + j % 4, at:at + P], xr[:, m, kt * P:(kt + 1) * P], ident)
                    mm.then_inc(xt_made, 1)

            def proj(q0, outs, one_bank=False, lo=0):
                for s in range(CK):
                    early_work(q0 + s)
                    pe.wait_ge(u_lo, (s + 1) * CK)
                    products(q0 + s, s, range(s * CK, (s + 1) * CK), lambda kt: normed(kt, lo), outs,
                             s == 0, s == CK - 1, one_bank)

            for i in range(2):
                if i:
                    pe.wait_ge(a_kept, i)
                proj(i * 2 * CK + Q_CONV, wide(0))
                if i:
                    pe.wait_ge(gate_sig, i)
                proj(i * 2 * CK + (Q_CONV + CK), wide(2))
            pe.wait_ge(a_kept, 2)
            proj(Q_POOL, wide(0))
            pe.wait_ge(xt_kept, NOB)
            proj(Q_POOL + CK, wide(pool_bank[1]))

            tiles_of = ((S0, META), (S1, P), (S2, 2 * P))

            def scores(n):
                g, t, half = n // HPG, n % HPG // 2, slice(n % 2 * DH, n % 2 * DH + DH)
                z = ps[:, 5 + n % 2, :]
                pe.wait_ge(k_kept, g + 1)
                pe.wait_ge(q_kept, g + 1)
                if g == 0:
                    pe.wait_ge(pads0, 2)
                if n >= 2:
                    pe.wait_ge(lw_done, n - 1)
                pe.wait_ge(vt_kept, 2 * (g + 1))
                for k, (at, t0) in enumerate(tiles_of):
                    mm = pe.matmul(z[:, at:at + TOK - t0], kb[g % 2][half, t, k * P:(k + 1) * P],
                                   qb[g % 2][half, t, t0 - META:SEQ], start=k == 0, stop=k == 2, skip_group_check=True)
                mm.then_inc(z_made, 1)

            def later_sums(n):
                z, s = ps[:, 5 + n % 2, :], sp[:, n % 2]
                pe.wait_ge(sp_done, n + 1)
                if n == 0:
                    pe.wait_ge(const_ready, 2)
                pe.matmul(z[:, 0:SM], negtri, s[:, 0:SM], start=False, stop=False, skip_group_check=True)
                pe.matmul(z[:, P - META:SEQ], negones, s[:, S1:S2], start=False, stop=False, skip_group_check=True)
                pe.matmul(z[:, S1 + P:S2], negones, s[:, S2:SM], start=False, stop=False, skip_group_check=True)
                pe.matmul(z[:, 2 * P - META:SEQ], negones, s[:, S2:SM], start=False, stop=True,
                          skip_group_check=True).then_inc(sum_made, 1)

            def values(n):
                g, t, e = n // HPG, n % HPG // 2, n % 2
                pe.wait_ge(wt_done, n + 1)
                if n % 2 == 0 and n >= 2:
                    pe.wait_ge(o_lo, n // 2)
                o = ps[e * DH:(e + 1) * DH, 7, t * SEQ:(t + 1) * SEQ]
                for k, (at, t0) in enumerate(tiles_of):
                    mm = pe.matmul(o[:, t0 - META:SEQ], vT[g % 2][:, k, t * P + e * DH:t * P + (e + 1) * DH],
                                   wt[:, n % 2, at:at + TOK - t0], start=k == 0, stop=k == 2, skip_group_check=True)
                mm.then_inc(o_made, 1)

            def side_work(q):
                if q - 4 in HEAD_AT:
                    values(HEAD_AT[q - 4])
                if q - 2 in HEAD_AT:
                    later_sums(HEAD_AT[q - 2])
                if q in HEAD_AT:
                    scores(HEAD_AT[q])
                if q in VT_AT:
                    g = VT_AT[q]
                    pe.wait_ge(v_kept, g + 1)
                    if g == 0:
                        pe.wait_ge(pm_done, NPG + 1)
                        pe.wait_ge(pads0, 2)
                    else:
                        pe.wait_ge(lw_done, HPG * g)
                    for m in range(2):
                        for k in range(3):
                            mm = pe.transpose(ps[:, 5 + m, k * P:(k + 1) * P], vb[g % 2][:, m, k * P:(k + 1) * P], ident)
                    mm.then_inc(vt_made, 1)
                if q == PE_MIX:
                    pe.wait_ge(sw_landed, 32)
                    pe.wait_ge(pu_kept, 2)
                    pe.wait_ge(pool_step, 2 * NPG)
                    for g in range(NPG):
                        mm = pe.matmul(ps[:, 5 + g // 2, (g % 2) * SEQ:(g % 2 + 1) * SEQ], wpl[:, g, :],
                                       pooled[:, g, :], start=True, stop=True)
                    mm.then_inc(mix_made, 1)
                if q == PE_SSP:
                    pe.wait_ge(pm_done, NPG + 1)
                    column_sums(ps[:, 7, 0:SEQ], [sq4[:, t, :] for t in range(PT)], ssp_made)
                if q == PE_LNM:
                    pe.wait_ge(tap_done, TAPS * CT)
                    pe.wait_ge(k_kept, (q - SC) // PER_G + 1)
                    column_sums(ps[:, 0, 0:SEQ], [cy[:, t, :] for t in range(CT)], lnm_made)
                if q == PE_LNV:
                    pe.wait_ge(ln_sq, 1)
                    column_sums(ps[:, 0, 0:SEQ], [sq4[:, t, :] for t in range(CT)], lnv_made)
                if q in (PE_PW, PE_PW + 1):
                    b = q - PE_PW
                    pe.wait_ge(ln_act, CT)
                    pe.wait_ge(k_kept, (PE_PW - SC) // PER_G + 1)
                    for m in range(2):
                        d0 = (2 * b + m) * P
                        for t in range(CT):
                            mm = pe.matmul(ps[:, b, m * SEQ:(m + 1) * SEQ], wpw[:, t, d0:d0 + P], mf[:, t, :],
                                           start=t == 0, stop=t == CT - 1)
                    mm.then_inc(pw_made, 1)
                if q == PE_SSC:
                    pe.wait_ge(oc_done, 2)
                    pe.wait_ge(v_kept, GROUPS)
                    column_sums(ps[:, 2, 0:SEQ], [sq4[:, t, :] for t in range(CT)], ssc_made)
                if q == PE_SSA:
                    pe.wait_ge(o_acc, DA // P)
                    pe.wait_ge(o_lo, DA // P)
                    column_sums(ps[:, 7, 0:SEQ], [acc_o], ssa_made)

            for g in range(GROUPS):
                for b, outs in enumerate((wide(2), two(4), wide(0))):
                    q0 = Q_ATT + g * PER_G + b * CK
                    if b == 0:
                        pe.wait_ge(gate_sig, 2)
                        if g:
                            pe.wait_ge(v_kept, g)
                    if b == 1:
                        pe.wait_ge(xt_kept, NOB)
                        if g:
                            pe.wait_ge(q_kept, g)
                    if b == 2:
                        pe.wait_ge(pu_kept, 1)
                        if g:
                            pe.wait_ge(k_kept, g)
                    if b == 2 and q0 > PE_PW:
                        pe.wait_ge(oc_done, 2)
                    if b == 2 and PE_LNV < q0 < PE_PW:
                        pe.wait_ge(ln_r, 1)
                    for s in range(CK):
                        side_work(q0 + s)
                        lo = META if b == 1 else 0
                        products(q0 + s, s, range(s * CK, (s + 1) * CK), lambda kt: normed(kt, lo), outs,
                                 s == 0, s == CK - 1, b == 1)

            y_of = {}
            for n, (part, j) in enumerate(out_parts):
                bank = (side_bank if part == "side" else attn_bank)[j]
                kt0 = DA // P if part == "side" else 0
                for s in range(OC):
                    q = Q_OUT + n * OC + s
                    side_work(q)
                    if s == 0:
                        if bank in y_of:
                            pe.wait_ge(y_done, y_of[bank] + 1)
                        elif part == "side":
                            pe.wait_ge((k_kept, k_kept, rc_done, v_kept, q_kept)[bank],
                                       (GROUPS, GROUPS, 1, GROUPS, GROUPS)[bank])
                        elif bank == 7:
                            pe.wait_ge(ra_done, 1)
                        else:
                            pe.wait_ge(lw_done, NH)
                        y_of[bank] = j
                    if part == "side":
                        pe.wait_ge(pool_lo, 1)
                        if s:
                            pe.wait_ge(conv_lo, 1)
                    else:
                        pe.wait_ge(o_lo, (s + 1) * CK)
                    products(q, q % WSLOTS, range(kt0 + s * CK, kt0 + (s + 1) * CK), merged, two(bank),
                             s == 0, s == OC - 1, True)

            pe.wait_ge(y_acc, NOB - 1)
            pe.wait_ge(y_sq, NOB)
            last = sqy[:, (NOB - 1) % 2]
            column_sums(ps[:, 1, 0:SEQ], [accy[:, 0, :], accy[:, 1, :], last[:, 0, :], last[:, 1, :]], ssy_made)
            for s in range(CK):
                pe.wait_ge(h2_lo, (s + 1) * CK)
                products(Q_FFN + s, s, range(s * CK, (s + 1) * CK), ffn_input, two(0), s == 0, s == CK - 1, True)

            def residual_work(s):
                if s == 1:
                    pe.wait_ge(h2_acc, NOB - 1)
                    column_sums(ps[:, 7, 0:SEQ], [accy[:, 0, :], accy[:, 1, :]], ss2_made)
                if s < 2:
                    return
                for n in range((s - 2) * DN, (s - 1) * DN):
                    m = n // DN
                    if n >= 4:
                        pe.wait_ge(rows_kept, n - 3)
                    for k in range(4):
                        kt = n % DN * 4 + k
                        mm = pe.transpose(ps[:, 2 + n % 4, k * P:(k + 1) * P], xT[:, kt, m * P:(m + 1) * P], ident)
                    mm.then_inc(rows_made, 1)

            def ffn_block(q0, bank, beside=None):
                for s in range(CK):
                    if beside:
                        beside(s)
                    products(q0 + s, s, range(s * CK, (s + 1) * CK), ffn_input, two(bank), s == 0, s == CK - 1, True)

            pe.wait_ge(r1_done, 1)
            ffn_block(Q_FFN + CK, 1, residual_work)
            with pe.Fori(1, NFB) as i:
                pe.wait_ge(gs_done, i)
                ffn_block(i * 2 * CK + Q_FFN, 0)
                pe.wait_ge(us_done, i)
                ffn_block(i * 2 * CK + (Q_FFN + CK), 1)

            with pe.Fori(0, DN // 2) as i:
                for b in range(2):
                    pe.wait_ge(down_free, i * 4 + (2 * b + 2))
                    for d in range(DCH):
                        slot = (b * DCH + d) % WSLOTS
                        pe.wait_ge(lo_done, i * 2 * DCH + (Q_DOWN + b * DCH + d + 1))
                        pe.wait_ge(f_lo, d + 1)
                        for k in range(2):
                            kt = 2 * d + k
                            mv = slice(k * DCOLS, (k + 1) * DCOLS)
                            for m in range(NQ):
                                o = ps[:, 2 + 2 * b + m, :]
                                rows_m = slice(m * P, (m + 1) * P)
                                first, last = d == 0 and k == 0, d == DCH - 1 and k == 1
                                pe.matmul(o, ffn[:, kt, 0, rows_m], w_hi[:, slot, mv], start=first, stop=False)
                                pe.matmul(o, ffn[:, kt, 0, rows_m], w_lo[:, slot, mv], start=False, stop=False)
                                mm = pe.matmul(o, ffn[:, kt, 1, rows_m], w_hi[:, slot, mv], start=False, stop=last)
                        mm.then_inc(chunks_used, 1)


_INS = ['x', 'meta_tokens', 'pre_mix_g', 'w_in', 'w_pool', 'pool_scale', 'w_dw', 'b_dw', 'conv_ln_g', 'conv_ln_b',
        'w_pw', 'mix_out_g', 'w_out', 'post_mix_g', 'pre_ffn_g', 'w_gate', 'w_up', 'w_down', 'post_ffn_g']


def kernel(**inputs):
    import numpy as np
    import concourse.bacc as bacc
    from concourse.bass_utils import run_bass_kernel_spmd

    nc = bacc.Bacc("TRN2", target_bir_lowering=False, num_devices=1)
    arrays, args = {}, []
    for name in _INS:
        a = np.ascontiguousarray(inputs[name])
        arrays[f"in_{name}"] = a
        args.append(nc.dram_tensor(f"in_{name}", a.shape, mybir.dt.from_np(a.dtype), kind="ExternalInput").ap())
    out = nc.dram_tensor("out", inputs["x"].shape, F32, kind="ExternalOutput").ap()
    build_trunk(nc, *args, out)
    r = run_bass_kernel_spmd(nc, [arrays], core_ids=[0])
    return r.results[0]["out"]
```

```python
from contextlib import ExitStack

import concourse.bass as bass
from concourse import mybir

F32 = mybir.dt.float32
F32R = mybir.dt.float32r
ALU = mybir.AluOpType
ACT = mybir.ActivationFunctionType
AX = mybir.AxisListType

P = 128
EPS = 1e-6
NEG = -1e30
WSLOTS = 4
CK = 4
BLK = 256
DCOLS = 512
LAG = 3
WARM_LOAD, WARM_ROWS, WARM_PARTS, WARM_FFN = 26, 10, 4, 30
POOL_TILES = 2


def build_trunk(nc, x, meta, pre_mix_g, w_in, w_pool, pool_scale, w_dw, b_dw, conv_ln_g, conv_ln_b, w_pw,
                mix_out_g, w_out, post_mix_g, pre_ffn_g, w_gate, w_up, w_down, post_ffn_g, out):
    _, SEQ, D = x.shape
    META = meta.shape[0]
    TOK = META + SEQ
    NQ = SEQ // P
    KT = D // P
    TAPS, DC = w_dw.shape[1], w_dw.shape[2]
    NPG, PG = w_pool.shape[1], w_pool.shape[2]
    DP = NPG * PG
    DA = D - DP - DC
    DH = 64
    FF = w_gate.shape[2]
    FT = FF // P
    CT = DC // P
    PT = DP // P
    KPAD = 3 * P
    GROUPS = DA // BLK
    HPG = BLK // DH
    assert NQ == 2 and P < TOK - P and TOK <= KPAD and PG == P

    Q_CONV = 0
    Q_POOL = Q_CONV + 4 * CK
    Q_ATT = Q_POOL + 2 * CK
    PER_G = 3 * CK
    Q_OUT = Q_ATT + GROUPS * PER_G
    FIRST = 5
    NOB = D // BLK
    Q_FFN = Q_OUT + NOB * CK
    NFB = FF // BLK
    Q_DOWN = Q_FFN + 2 * CK * NFB
    DN = D // DCOLS
    DCH = FT // 2
    SC = (Q_ATT + PER_G)
    C_POOL, C_A, C_GATE = 3 * DA, 3 * DA + DP, 3 * DA + DP + DC

    def attn_at(n):
        g, h = n // HPG, n % HPG
        if g == GROUPS - 1:
            return Q_OUT + 1 + h + h // 2
        return SC + PER_G * g + 1 + 2 * h
    NH = GROUPS * HPG
    HEAD_AT = {attn_at(n): n for n in range(NH)}
    VT_AT = {SC + PER_G * g - 1: g for g in range(GROUPS)}
    Q_TAPS = Q_POOL + CK
    VT = CT - POOL_TILES
    VEC_AT, TURN_AT = 3, 4
    PE_MIX = Q_POOL + 12
    PE_SSP = Q_POOL + 16
    PE_LNM = Q_TAPS + TAPS - 1
    PE_LNV = PE_LNM + 4
    PE_PW = PE_LNV + 9
    PE_SSC = PE_PW + 6
    PE_SSA = Q_OUT + 12

    out_parts = [("side", j) for j in range(FIRST)] + [("attn", j) for j in range(FIRST)] + \
                [("side", j) for j in range(FIRST, NOB - 1)] + [("attn", j) for j in range(FIRST, NOB)] + \
                [("side", NOB - 1)]
    OC = CK // 2
    side_bank = [4, 3, 2, 0, 1, 2, 0, 1]
    attn_bank = [5, 6, 7, 4, 3, 5, 6, 7]
    pool_bank = [0, 5]
    T_AT = {Q_OUT + OC * n + OC - 1 + 4: j for n, (part, j) in enumerate(out_parts) if part == "attn"}
    Y_AT = {(at if j < NOB - 1 else Q_FFN - 1 + 4): j for at, j in T_AT.items()}

    OUT_PIECES = [(0, slice(0, D // 8)), (0, slice(D // 8, D // 2)), (0, slice(D // 2, D)),
                  (1, slice(0, D // 2)), (1, slice(D // 2, D))]

    with ExitStack() as ctx:
        top = [(nc.sbuf_base + 63) // 64 * 64]

        def place(nbytes):
            at = top[0]
            top[0] += nbytes
            return at

        def sb_at(name, shape, dt, at):
            return nc.alloc_sbuf_tensor_at(name, shape, dt, offset=at)

        CE = CK * BLK
        raw = sb_at("raw", [P, WSLOTS, CE], F32, place(4 * WSLOTS * CE))
        w_hi = sb_at("w_hi", [P, WSLOTS, CE], F32R, place(4 * WSLOTS * CE))
        w_lo = sb_at("w_lo", [P, WSLOTS, CE], F32R, place(4 * WSLOTS * CE))
        a_in = place(4 * KT * 2 * TOK)
        u = sb_at("u", [P, KT, 2, TOK], F32R, a_in)
        f_acc = sb_at("f_acc", [P, NQ, D], F32, a_in)
        a_xt = place(4 * KT * SEQ)
        xT = sb_at("xT", [P, KT, SEQ], F32, a_xt)
        gbc = sb_at("gbc", [P, D], F32, a_xt)
        tmp_ffn = sb_at("tmp_ffn", [P, 4, 2 * SEQ], F32, a_xt + 4 * D)
        xs = sb_at("xs", [P, NQ, D], F32, a_xt)
        a_y = place(4 * KT * SEQ)
        y = sb_at("y", [P, KT, SEQ], F32, a_y)
        h2rows = sb_at("h2rows", [P, NQ, D], F32, a_y)
        side = sb_at("side", [P, KT * SEQ], F32, a_y)
        a_c = place(4 * 1152)
        cst = sb_at("cst", [P, 1152], F32, a_c)
        a_ff = place(4 * FT * 2 * SEQ)
        ffn = sb_at("ffn", [P, FT, 2, SEQ], F32R, a_ff)
        AR = (FT - KT) * 2 * SEQ
        arena = sb_at("arena", [P, AR], F32, a_ff + 4 * KT * 2 * SEQ)
        assert top[0] <= nc.sbuf_usable_end

        def carve(tensor, at, *dims):
            n = 1
            for d in dims:
                n *= d
            ap = tensor[:, at:at + n]
            if len(dims) == 2:
                ap = ap.rearrange("p (a b) -> p a b", a=dims[0])
            if len(dims) == 3:
                ap = ap.rearrange("p (a b c) -> p a b c", a=dims[0], b=dims[1])
            return ap, at + n

        ident, c = carve(cst, 0, P)
        ones, c = carve(cst, c, P)
        NV = 4 * KT + PT + 3 * CT
        NB = NV - KT
        vec, c = carve(cst, c, NV)
        dw, c = carve(cst, c, TAPS * CT)
        eps, c = carve(cst, c, 1)
        ss0, c = carve(cst, c, 3)
        r0, c = carve(cst, c, 3)
        ssd, c = carve(cst, c, NQ, DN)
        sst, c = carve(cst, c, NQ)
        rd, c = carve(cst, c, NQ)
        r2, c = carve(cst, c, SEQ)
        assert c <= 1152
        V_PRE, V_MIX, V_POST, V_FFN = 0, KT, 2 * KT, 3 * KT
        V_PS, V_BDW = 4 * KT, 4 * KT + PT
        V_LNG, V_LNB = V_BDW + CT, V_BDW + 2 * CT
        wpw, c = carve(side, 0, CT, DC)
        wpl, c = carve(side, c, NPG, PG)
        sq4, c = carve(side, c, CT, SEQ)
        acc_o, c = carve(side, c, SEQ)
        sq_o, c = carve(side, c, SEQ)
        assert c <= KT * SEQ
        GP = TAPS - 1
        SM = TOK - META + (TOK - P) + (TOK - 2 * P)
        S0, S1, S2 = 0, TOK - META, TOK - META + TOK - P
        glu, c = carve(arena, 0, CT, GP + TOK)
        xsm = arena[:, c:c + D]
        cy, c = carve(arena, c, CT, SEQ)
        mf, c = carve(arena, c, CT, SEQ)
        mask, c = carve(arena, c, SM)
        negtri, c = carve(arena, c, P)
        negones, c = carve(arena, c, P)
        rside, c = carve(arena, c, SEQ)
        ra, c = carve(arena, c, SEQ)
        qb, kb, vb, vT = [None] * 2, [None] * 2, [None] * 2, [None] * 2
        grow, e = carve(arena, c, P)
        vrow, e = carve(arena, e, P)
        drow, e = carve(arena, e, P)
        a_s, e = carve(arena, e, 2, TOK)
        sg, e = carve(arena, e, 2, TOK)
        assert e - c <= 2 * SEQ + 4 * KPAD + 3 * BLK
        qb[0], c = carve(arena, c, 2, SEQ)
        kb[0], c = carve(arena, c, 2, KPAD)
        vb[0], c = carve(arena, c, 2, KPAD)
        vT[0], c = carve(arena, c, 3, BLK)
        over = c
        qb[1], c = carve(arena, c, 2, SEQ)
        kb[1], c = carve(arena, c, 2, KPAD)
        vb[1], c = carve(arena, c, 2, KPAD)
        vT[1], c = carve(arena, c, 3, BLK)
        zm, c = carve(arena, c, 2, SM)
        lg, c = carve(arena, c, SM)
        sp, c = carve(arena, c, 2, SM)
        wt, c = carve(arena, c, 4, SM)
        assert c <= AR
        ptmp, c = carve(arena, c, POOL_TILES, SEQ)
        xr, e = carve(arena, over, 3, D)
        assert e <= c
        pu, e = carve(arena, over, PT, TOK)
        pw0, e = carve(arena, e, PT, TOK)
        pw1, e = carve(arena, e, PT, TOK)
        pooled, e = carve(arena, e, PT, SEQ)
        assert e <= c
        tb, e = carve(arena, over, 2, SEQ)
        sqy, e = carve(arena, e, 2, 2, SEQ)
        accy, e = carve(arena, e, 2, SEQ)
        r1, e = carve(arena, e, SEQ)
        th, e = carve(arena, e, 2, 2, SEQ)
        assert e <= AR
        sqh, e = carve(arena, 0, KT // 2, 2 * SEQ)
        assert e <= over

        ps = ctx.enter_context(nc.psum_tensor("ps", [P, 8, 512], F32))

        def sem(name):
            return ctx.enter_context(nc.semaphore(name))

        slot_free = sem("slot_free")
        raw_landed = [sem(f"raw_landed{s}") for s in range(WSLOTS)]
        hi_done, lo_done, chunks_used = sem("hi_done"), sem("lo_done"), sem("chunks_used")
        x_landed = [sem(f"x_landed{m}") for m in range(3)]
        grow_landed, vec_landed, sw_landed, gbc_landed, stored = (
            sem("grow_landed"), sem("vec_landed"), sem("sw_landed"), sem("gbc_landed"), sem("stored"))
        const_step, const_ready, pads_ready, pads0, lg_done = (
            sem("const_step"), sem("const_ready"), sem("pads_ready"), sem("pads0"), sem("lg_done"))
        ss_dve, ss_act, r0_done, xs_dve, xs_act = (
            sem("ss_dve"), sem("ss_act"), sem("r0_done"), sem("xs_dve"), sem("xs_act"))
        grow_turned, grow_done, vec_turned, vec_done, u_made, xt_made, xt_kept, u_hi, u_lo = (
            sem("grow_turned"), sem("grow_done"), sem("vec_turned"), sem("vec_done"), sem("u_made"), sem("xt_made"),
            sem("xt_kept"), sem("u_hi"), sem("u_lo"))
        a_kept, gate_sig, glu_done, tap_done = sem("a_kept"), sem("gate_sig"), sem("glu_done"), sem("tap_done")
        pu_kept, pool_step, mix_made, pm_done, ssp_made, rp_done, pn_done, pool_hi, pool_lo = (
            sem("pu_kept"), sem("pool_step"), sem("mix_made"), sem("pm_done"), sem("ssp_made"), sem("rp_done"),
            sem("pn_done"), sem("pool_hi"), sem("pool_lo"))
        lnm_made, ln_cent, ln_sq, lnv_made, ln_r, ln_y, ln_act, pw_made, oc_done, ssc_made, rc_done, cn_done, \
            conv_hi, conv_lo = (sem(n) for n in ("lnm_made", "ln_cent", "ln_sq", "lnv_made", "ln_r", "ln_y", "ln_act",
                                                 "pw_made", "oc_done", "ssc_made", "rc_done", "cn_done",
                                                 "conv_hi", "conv_lo"))
        v_kept, q_kept, k_kept, vt_made, vt_kept = (
            sem("v_kept"), sem("q_kept"), sem("k_kept"), sem("vt_made"), sem("vt_kept"))
        z_made, zm_done, log_step, sp_done, sum_made, lw_done, wt_done, o_made, o_sq, o_hi, o_acc, o_lo = (
            sem(n) for n in ("z_made", "zm_done", "log_step", "sp_done", "sum_made", "lw_done", "wt_done", "o_made",
                             "o_sq", "o_hi", "o_acc", "o_lo"))
        ssa_made, ra_done, t_done, y_done, y_sq, y_gain, y_acc = (
            sem(n) for n in ("ssa_made", "ra_done", "t_done", "y_done", "y_sq", "y_gain", "y_acc"))
        tiles_added, pool_tap = sem("tiles_added"), sem("pool_tap")
        ssy_made, r1_done, th_done, h2_done, h2_hi, h2_lo, h2_sq, h2_acc, ss2_made, r2_done, rows_made, rows_kept = (
            sem(n) for n in ("ssy_made", "r1_done", "th_done", "h2_done", "h2_hi", "h2_lo", "h2_sq", "h2_acc",
                             "ss2_made", "r2_done", "rows_made", "rows_kept"))
        gs_done, silu_done, us_done, p_done, f_hi, f_lo = (
            sem(n) for n in ("gs_done", "silu_done", "us_done", "p_done", "f_hi", "f_lo"))
        down_free, dsq_done, f_done, sst_done, rd_done, res_done = (
            sem(n) for n in ("down_free", "dsq_done", "f_done", "sst_done", "rd_done", "res_done"))

        def tiles(w):
            return w.rearrange("a (kt p) n -> p (a kt) n", p=P)

        win_v, wout_v, wg_v, wu_v, wd_v = tiles(w_in), tiles(w_out), tiles(w_gate), tiles(w_up), tiles(w_down)
        out_v = out.rearrange("a (m p) d -> p (a m) d", p=P)

        block = ctx.enter_context(nc.Block())

        @block.sync
        def _(sp_eng):
            sp_eng.dma_start(xr[0:META, 2, :], meta).then_inc(x_landed[2], 16)
            for m in range(NQ):
                sp_eng.dma_start(xr[:, m, :], x[0, m * P:(m + 1) * P, :]).then_inc(x_landed[m], 16)
            sp_eng.dma_start(grow[0:KT, :], pre_mix_g.rearrange("a (c p) -> (a c) p", p=P)).then_inc(grow_landed, 16)

            def load(src, kt, n0, q, slot, kts=CK, cols=BLK, wait=True):
                if wait:
                    sp_eng.wait_ge(lo_done, q - WSLOTS + 1)
                    if not isinstance(q, int):
                        sp_eng.sem_inc(slot_free, 1)
                sp_eng.dma_start(raw[:, slot, :].rearrange("p (k n) -> p k n", k=kts),
                                 src[:, kt:kt + kts, bass.ds(n0, cols)]).then_inc(raw_landed[slot], 16)

            for i in range(2):
                for b, col in enumerate((C_A, C_GATE)):
                    for s in range(CK):
                        q = Q_CONV + (2 * i + b) * CK + s
                        load(win_v, s * CK, col + i * BLK, q, s, wait=q >= WSLOTS)
            with sp_eng.Fori(0, 2) as i:
                for s in range(CK):
                    load(win_v, s * CK, C_POOL + i * BLK, i * CK + (Q_POOL + s), s)
            with sp_eng.Fori(0, GROUPS) as g:
                for b, col in enumerate((2 * DA, 0, DA)):
                    for s in range(CK):
                        load(win_v, s * CK, col + g * BLK, g * PER_G + (Q_ATT + b * CK + s), s)
            for n, (part, j) in enumerate(out_parts):
                for s in range(OC):
                    q = Q_OUT + n * OC + s
                    kt = (DA // P if part == "side" else 0) + s * CK
                    load(wout_v, kt, j * BLK, q, q % WSLOTS)
            for s in range(CK):
                for b, src in enumerate((wg_v, wu_v)):
                    q = Q_FFN + 2 * s + b
                    load(src, s * CK, 0, q, q % WSLOTS)
            with sp_eng.Fori(1, NFB) as i:
                for b, src in enumerate((wg_v, wu_v)):
                    for s in range(CK):
                        load(src, s * CK, i * BLK, i * 2 * CK + (Q_FFN + b * CK + s), s)
            with sp_eng.Fori(0, DN // 2) as i:
                for b in range(2):
                    for d in range(DCH):
                        load(wd_v, 2 * d, i * 2 * DCOLS + b * DCOLS, i * 2 * DCH + (Q_DOWN + b * DCH + d),
                             (b * DCH + d) % WSLOTS, kts=2, cols=DCOLS)
            for n, (m, cols) in enumerate(OUT_PIECES):
                sp_eng.wait_ge(res_done, n + 1)
                sp_eng.dma_start(out_v[:, m, cols], f_acc[:, m, cols]).then_inc(stored, 16)
            sp_eng.wait_ge(stored, 16 * len(OUT_PIECES))

        @block.gpsimd
        def _(pool):
            pool.memset(ident, 0.0).then_inc(const_step, 1)
            pool.memset(ones, 1.0).then_inc(const_step, 1)
            pool.memset(eps, EPS).then_inc(const_step, 1)
            pool.memset(negtri, -1.0).then_inc(const_step, 1)
            pool.memset(negones, -1.0).then_inc(const_step, 1)
            pool.memset(mask, 0.0).then_inc(const_step, 1)
            pool.wait_ge(const_step, 6)
            pool.affine_select(ident, ident, [[-1, P]], ALU.not_equal, 1.0, base=0,
                               channel_multiplier=1).then_inc(const_ready, 1)
            pool.affine_select(negtri, negtri, [[-1, P]], ALU.is_ge, 0.0, base=0,
                               channel_multiplier=1).then_inc(const_ready, 1)
            for at, n, base in ((S0, P - META, META), (S1, P, 0), (S2, TOK - 2 * P, 0)):
                pool.affine_select(mask[:, at:at + n], mask[:, at:at + n], [[1, n]], ALU.is_gt, NEG, base=base,
                                   channel_multiplier=-1).then_inc(const_ready, 1)
            at = 0
            for v in (mix_out_g, post_mix_g, pre_ffn_g, pool_scale, b_dw, conv_ln_g, conv_ln_b):
                n = v.shape[1] // P
                pool.dma_start(vrow[at:at + n, :], v.rearrange("a (c p) -> (a c) p", p=P)).then_inc(vec_landed, 16)
                at += n
            pool.dma_start(drow[0:TAPS * CT, :], w_dw.rearrange("a w (c p) -> (a w c) p", p=P)).then_inc(vec_landed, 16)
            pool.dma_start(wpl, w_pool.rearrange("a g c d -> c (a g) d")).then_inc(sw_landed, 16)
            pool.dma_start(wpw, w_pw.rearrange("a (c p) n -> p (a c) n", p=P)).then_inc(sw_landed, 16)
            pool.memset(glu[:, :, 0:GP], 0.0).then_inc(pads_ready, 1)
            pool.wait_ge(glu_done, 2)
            pool.memset(kb[0][:, :, TOK:KPAD], 0.0).then_inc(pads0, 1)
            pool.memset(vb[0][:, :, TOK:KPAD], 0.0).then_inc(pads0, 1)

            def taps(ws):
                for w in ws:
                    tap = dw[:, w * CT + VT:(w + 1) * CT].rearrange("p (t o) -> p t o", o=1)
                    if w:
                        pool.wait_ge(pool_tap, 2 * w)
                    pool.tensor_tensor(ptmp, glu[:, VT:CT, META + w:META + w + SEQ],
                                       tap.to_broadcast([P, POOL_TILES, SEQ]), ALU.mult).then_inc(pool_tap, 1)
                    bias = vec[:, V_BDW + VT:V_BDW + CT].rearrange("p (t o) -> p t o", o=1)
                    before = cy[:, VT:CT, :] if w else bias.to_broadcast([P, POOL_TILES, SEQ])
                    pool.wait_ge(pool_tap, 2 * w + 1)
                    pool.tensor_tensor(cy[:, VT:CT, :], ptmp, before, ALU.add).then_inc(pool_tap, 1)

            pool.wait_ge(vec_done, 2)
            pool.wait_ge(pads_ready, 1)
            taps(range(0, TAPS // 2))
            pool.wait_ge(pm_done, NPG + 1)
            pool.tensor_tensor(sq4[:, 0:2, :], sq4[:, 0:2, :], sq4[:, 2:4, :], ALU.add).then_inc(tiles_added, 1)
            pool.wait_ge(tiles_added, 1)
            pool.tensor_tensor(sq4[:, 0, :], sq4[:, 0, :], sq4[:, 1, :], ALU.add).then_inc(tiles_added, 1)
            pool.wait_ge(pn_done, PT)
            pool.memset(kb[1][:, :, TOK:KPAD], 0.0).then_inc(pads_ready, 1)
            pool.memset(vb[1][:, :, TOK:KPAD], 0.0).then_inc(pads_ready, 1)

            taps(range(TAPS // 2, TAPS))

            def add_tiles(src, n):
                pool.tensor_tensor(sq4[:, 0:2, :], src[:, 0:2, :], src[:, 2:4, :], ALU.add).then_inc(tiles_added, 1)
                pool.wait_ge(tiles_added, 2 * n - 1)
                pool.tensor_tensor(sq4[:, 0, :], sq4[:, 0, :], sq4[:, 1, :], ALU.add).then_inc(tiles_added, 1)

            pool.wait_ge(ssp_made, 1)
            pool.wait_ge(tap_done, TAPS * VT)
            pool.wait_ge(pool_tap, 2 * TAPS)
            add_tiles(cy, 2)
            pool.wait_ge(ln_sq, 1)
            add_tiles(sq4, 3)
            pool.wait_ge(oc_done, 2)
            add_tiles(sq4, 4)
            acc2 = accy.rearrange("p a t -> p (a t)")
            for j in range(1, NOB):
                pool.wait_ge(h2_sq, j + 1)
                if j >= 2:
                    pool.wait_ge(h2_acc, j - 1)
                pool.tensor_tensor(acc2, sqh[:, 0, :] if j == 1 else acc2, sqh[:, j, :], ALU.add).then_inc(h2_acc, 1)

        def hi_view(ap):
            return ap.bitcast(F32)

        @block.scalar
        def _(act):
            def split_hi(q, slot, turn):
                act.wait_ge(raw_landed[slot], 16 * (turn + 1))
                if not isinstance(q, int) or q >= WSLOTS:
                    act.wait_ge(chunks_used, q - WSLOTS + 1)
                act.activation(w_hi[:, slot, :], raw[:, slot, :], ACT.Copy).then_inc(hi_done, 1)

            def split(q):
                split_hi(q, q % WSLOTS, q // WSLOTS)

            step = [0]

            def inv_rms(dst, src, n, done):
                act.activation(dst, src, ACT.Ln, bias=eps[0:dst.shape[0]], scale=1.0 / n).then_inc(log_step, 1)
                step[0] += 1
                act.wait_ge(log_step, step[0])
                act.activation(dst, dst, ACT.Exp, scale=-0.5).then_inc(done, 1)

            act.preload_act_table_set("natural_log_exp_and_others")
            act.wait_ge(const_step, 6)
            act.wait_ge(x_landed[2], 16)
            act.activation(xsm[0:META], xr[0:META, 2, :], ACT.Square, accum_out=ss0[0:META, 2:3]).then_inc(ss_act, 1)
            act.wait_ge(ss_act, 1)
            inv_rms(r0[0:META, 2:3], ss0[0:META, 2:3], D, r0_done)
            act.wait_ge(r0_done, 1)
            act.activation(xsm[0:META], xr[0:META, 2, :], ACT.Copy, scale=r0[0:META, 2:3]).then_inc(xs_act, 1)
            act.wait_ge(x_landed[1], 16)
            act.activation(xs[:, 1, 0:D // 2], xr[:, 1, 0:D // 2], ACT.Square, accum_out=ss0[:, 1:2]).then_inc(ss_act, 1)
            act.wait_ge(ss_dve, 3)
            inv_rms(r0[:, 0:2], ss0[:, 0:2], D, r0_done)
            act.wait_ge(r0_done, 2)
            act.activation(xs[:, 1, 0:D // 2], xr[:, 1, 0:D // 2], ACT.Copy, scale=r0[:, 1:2]).then_inc(xs_act, 1)
            act.wait_ge(grow_turned, 1)
            act.copy(vec[:, 0:KT], ps[:, 0, 0:KT]).then_inc(grow_done, 1)
            act.wait_ge(grow_done, 1)
            for kt in range(KT):
                act.wait_ge(u_made, kt + 1)
                act.activation(u[:, kt, 0, :], ps[:, 4 + kt % 4, 0:TOK], ACT.Copy,
                               scale=vec[:, V_PRE + kt:V_PRE + kt + 1]).then_inc(u_hi, 1)
                if kt % CK == CK - 1:
                    split(kt // CK)

            def soft(n):
                act.wait_ge(zm_done, n + 1)
                if n >= 1:
                    act.wait_ge(sp_done, n)
                act.activation(lg, zm[:, n % 2], ACT.Abs).then_inc(log_step, 1)
                step[0] += 1
                act.wait_ge(log_step, step[0])
                act.activation(lg, lg, ACT.Exp, scale=-1.0).then_inc(log_step, 1)
                step[0] += 1
                act.wait_ge(log_step, step[0])
                act.activation(lg, lg, ACT.Ln, bias=1.0).then_inc(lg_done, 1)

            def weights(n):
                act.wait_ge(lw_done, n + 1)
                act.activation(wt[:, n % 4], wt[:, n % 4], ACT.Exp).then_inc(wt_done, 1)

            def head_pair_out(n):
                kt = n // 2
                o = ps[:, 7, (kt % 2) * SEQ:(kt % 2 + 1) * SEQ]
                act.wait_ge(o_made, kt + 1)
                if kt >= 1:
                    act.wait_ge(o_acc, kt)
                act.activation(sq_o, o, ACT.Square).then_inc(o_sq, 1)
                act.activation(ffn[:, kt, 0, :], o, ACT.Copy, scale=vec[:, V_MIX + kt:V_MIX + kt + 1]).then_inc(o_hi, 1)

            def y_squares(j):
                act.wait_ge(y_done, j + 1)
                if j >= 2:
                    act.wait_ge(y_acc, j - 1)
                act.activation(sqy[:, j % 2], y[:, 2 * j:2 * j + 2, :], ACT.Square).then_inc(y_sq, 1)

            def y_gains(j):
                act.wait_ge(y_sq, j + 1)
                for kt in (2 * j, 2 * j + 1):
                    act.activation(y[:, kt, :], y[:, kt, :], ACT.Copy,
                                   scale=vec[:, V_POST + kt:V_POST + kt + 1]).then_inc(y_gain, 1)

            for q in range(WSLOTS, Q_FFN + CK):
                if q < Q_FFN + CK - 1:
                    split(q)
                e = q - 4
                if q == VEC_AT + LAG:
                    act.wait_ge(vec_turned, 1)
                    act.copy(vec[:, KT:NV], ps[:, 7, 0:NB]).then_inc(vec_done, 1)
                    act.copy(dw, ps[:, 7, P:P + TAPS * CT]).then_inc(vec_done, 1)
                if 0 <= q - LAG - TURN_AT < NOB:
                    j = q - LAG - TURN_AT
                    act.wait_ge(xt_made, j + 1)
                    if j == 0:
                        act.wait_ge(u_made, KT)
                    act.copy(xT[:, 2 * j:2 * j + 2, :],
                             ps[:, 4 + j % 4, :].rearrange("p (a t) -> p a t", a=2)).then_inc(xt_kept, 1)
                for i in range(2):
                    if e == Q_CONV + 2 * i * CK + CK - 1:
                        act.wait_ge(chunks_used, e + 1)
                        if i:
                            act.wait_ge(glu_done, 1)
                        act.copy(a_s, ps[:, 0:2, 0:TOK]).then_inc(a_kept, 1)
                    if e == Q_CONV + 2 * i * CK + 2 * CK - 1:
                        act.wait_ge(chunks_used, e + 1)
                        act.activation(sg, ps[:, 2:4, 0:TOK], ACT.Sigmoid).then_inc(gate_sig, 1)
                        act.preload_act_table_set("natural_log_exp_and_others")
                    if e == Q_POOL + (i + 1) * CK - 1:
                        act.wait_ge(chunks_used, e + 1)
                        if i == 0:
                            act.wait_ge(xt_made, NOB)
                        b = pool_bank[i]
                        act.copy(pu[:, 2 * i:2 * i + 2, :], ps[:, b:b + 2, 0:TOK]).then_inc(pu_kept, 1)
                if Q_ATT <= e < Q_OUT:
                    g, b = (e - Q_ATT) // PER_G, (e - Q_ATT) % PER_G
                    if b % CK == CK - 1:
                        act.wait_ge(chunks_used, e + 1)
                        if b < CK:
                            if g == 1:
                                act.wait_ge(pads_ready, 3)
                            if g >= 2:
                                act.wait_ge(vt_made, g - 1)
                            act.copy(vb[g % 2][:, :, 0:TOK], ps[:, 2:4, 0:TOK]).then_inc(v_kept, 1)
                        elif b < 2 * CK:
                            if g >= 2:
                                act.wait_ge(z_made, HPG * (g - 1))
                            act.mul(qb[g % 2], ps[:, 4, :].rearrange("p (m t) -> p m t", m=2),
                                    DH ** -0.5).then_inc(q_kept, 1)
                        else:
                            if g >= 2:
                                act.wait_ge(z_made, HPG * (g - 1))
                            act.copy(kb[g % 2][:, :, 0:TOK], ps[:, 0:2, 0:TOK]).then_inc(k_kept, 1)
                if q - LAG in VT_AT:
                    g = VT_AT[q - LAG]
                    act.wait_ge(vt_made, g + 1)
                    if g >= 2:
                        act.wait_ge(o_made, HPG // 2 * (g - 1))
                    for m in range(2):
                        act.copy(vT[g % 2][:, :, m * P:(m + 1) * P],
                                 ps[:, 5 + m, 0:KPAD].rearrange("p (k d) -> p k d", k=3)).then_inc(vt_kept, 1)
                if q - 5 in HEAD_AT:
                    weights(HEAD_AT[q - 5])
                if q - 3 in HEAD_AT:
                    soft(HEAD_AT[q - 3])
                if q - 7 in HEAD_AT and HEAD_AT[q - 7] % 2:
                    head_pair_out(HEAD_AT[q - 7])

                if q == PE_MIX + LAG:
                    act.wait_ge(mix_made, 1)
                    for g in range(NPG):
                        act.activation(mf[:, g, :], ps[:, 5 + g // 2, (g % 2) * SEQ:(g % 2 + 1) * SEQ], ACT.Copy,
                                       scale=vec[:, V_PS + g:V_PS + g + 1]).then_inc(pm_done, 1)
                    act.wait_ge(pm_done, NPG)
                    act.activation(sq4, mf, ACT.Square).then_inc(pm_done, 1)
                if q == PE_SSP + LAG:
                    act.wait_ge(ssp_made, 1)
                    inv_rms(rside, ps[:, 7, 0:SEQ], DP, rp_done)
                if q == PE_SSP + LAG + 1:
                    act.wait_ge(pn_done, PT)
                    act.copy(ffn[:, DA // P:DA // P + PT, 0, :], mf).then_inc(pool_hi, 1)

                if q == PE_LNM + LAG + 1:
                    act.wait_ge(ln_cent, CT)
                    act.activation(sq4, cy, ACT.Square).then_inc(ln_sq, 1)
                if q == PE_LNV + LAG:
                    act.wait_ge(lnv_made, 1)
                    act.wait_ge(pn_done, PT)
                    inv_rms(rside, ps[:, 0, 0:SEQ], DC, ln_r)
                if q == PE_LNV + LAG + 2:
                    act.wait_ge(ln_y, CT)
                    act.wait_ge(pool_lo, 1)
                    for t in range(CT):
                        act.activation(mf[:, t, :], cy[:, t, :], ACT.Silu,
                                       bias=vec[:, V_LNB + t:V_LNB + t + 1]).then_inc(ln_act, 1)
                    act.preload_act_table_set("natural_log_exp_and_others")
                if q == PE_PW + LAG + 1:
                    act.wait_ge(pw_made, 2)
                    act.copy(cy, ps[:, 0:2, :].rearrange("p b (c t) -> p (b c) t", c=2)).then_inc(oc_done, 1)
                    act.activation(sq4, ps[:, 0:2, :].rearrange("p b (c t) -> p (b c) t", c=2),
                                   ACT.Square).then_inc(oc_done, 1)
                if q == PE_SSC + LAG:
                    act.wait_ge(ssc_made, 1)
                    inv_rms(rside, ps[:, 2, 0:SEQ], DC, rc_done)
                if q == PE_SSC + LAG + 1:
                    act.wait_ge(cn_done, CT)
                    act.copy(ffn[:, (DA + DP) // P:KT, 0, :], mf).then_inc(conv_hi, 1)

                if q == PE_SSA + LAG:
                    act.wait_ge(ssa_made, 1)
                    inv_rms(ra, ps[:, 7, 0:SEQ], DA, ra_done)
                if q - 1 in Y_AT:
                    y_squares(Y_AT[q - 1])
                    y_gains(Y_AT[q - 1])

            y_squares(NOB - 1)
            split(Q_FFN + CK - 1)
            act.wait_ge(ssy_made, 1)
            inv_rms(r1, ps[:, 2, 0:SEQ], D, r1_done)
            y_gains(NOB - 1)

            def keep_rows(n):
                c, m = n // NQ, n % NQ
                act.wait_ge(rows_made, n + 1)
                act.wait_ge(th_done, m * NOB // 2 + c + 1)
                act.copy(h2rows[:, m, c * DCOLS:(c + 1) * DCOLS], ps[:, 3 + n % 4, :]).then_inc(rows_kept, 1)

            for j in range(NOB):
                act.wait_ge(h2_done, j + 1)
                for kt in (2 * j, 2 * j + 1):
                    act.activation(u[:, kt, 0, 0:SEQ], xT[:, kt, :], ACT.Copy,
                                   scale=vec[:, V_FFN + kt:V_FFN + kt + 1]).then_inc(h2_hi, 1)
                act.activation(sqh[:, j, :], xT[:, 2 * j:2 * j + 2, :].rearrange("p a t -> p (a t)"),
                               ACT.Square).then_inc(h2_sq, 1)
                if j >= NOB // 2:
                    split(Q_FFN + WSLOTS + j - NOB // 2)
                    keep_rows(j - NOB // 2)
            split(Q_FFN + 2 * CK)
            keep_rows(4)
            keep_rows(5)
            act.wait_ge(ss2_made, 1)
            inv_rms(r2, ps[:, 7, 0:SEQ], D, r2_done)
            split(Q_FFN + 2 * CK + 1)
            split(Q_FFN + 2 * CK + 2)

            def silu(i):
                act.wait_ge(gs_done, i + 1)
                act.activation(tmp_ffn[:, 1, :], tmp_ffn[:, 0, :], ACT.Silu).then_inc(silu_done, 1)

            keep_rows(6)
            keep_rows(7)
            act.wait_ge(rows_kept, 2 * DN)
            act.sem_inc(down_free, 4)
            act.dma_start(gbc[:, :], post_ffn_g.to_broadcast([P, D])).then_inc(gbc_landed, 16)
            silu(0)
            for s in range(3, 2 * CK):
                split(Q_FFN + 2 * CK + s)

            silu0 = Q_FFN + 2 * CK
            with act.Fori(1, NFB - 1) as i:
                silu(i)
                for s in range(2 * CK):
                    split_hi(i * 2 * CK + (silu0 + s), s % WSLOTS, i * 2 + (silu0 + s) // WSLOTS)
            silu(NFB - 1)

            for q in range(Q_DOWN, Q_DOWN + DN * DCH + 4):
                if q < Q_DOWN + DN * DCH:
                    split(q)
                if q == Q_DOWN + 4:
                    act.preload_act_table_set("natural_log_exp_and_others")
                n, rest = (q - 4 - Q_DOWN) // DCH, (q - 4 - Q_DOWN) % DCH
                if q - 4 >= Q_DOWN and rest == DCH - 1:
                    act.wait_ge(chunks_used, q - 3)
                    for m in range(NQ):
                        if n or m:
                            act.wait_ge(dsq_done, NQ * n + m)
                        if m:
                            act.wait_ge(f_done, NQ * n + 1)
                        act.activation(tmp_ffn[:, 0, :], ps[:, 2 + 2 * (n % 2) + m, :], ACT.Square,
                                       accum_out=ssd[:, m, n:n + 1]).then_inc(dsq_done, 1)
                    act.wait_ge(dsq_done, NQ * (n + 1))
                    act.sem_inc(down_free, 1)
            act.wait_ge(sst_done, 1)
            inv_rms(rd, sst, D, rd_done)

        @block.vector
        def _(dve):
            def split_lo(q, slot):
                dve.wait_ge(hi_done, q + 1)
                dve.tensor_tensor(w_lo[:, slot, :], raw[:, slot, :], hi_view(w_hi[:, slot, :]),
                                  ALU.subtract).then_inc(lo_done, 1)

            def split(q):
                split_lo(q, q % WSLOTS)

            dve.wait_ge(x_landed[0], 16)
            dve.scalar_tensor_tensor(xs[:, 0, :], xr[:, 0, :], 1.0, xr[:, 0, :], ALU.mult, ALU.mult,
                                     accum_out=ss0[:, 0:1]).then_inc(ss_dve, 1)
            dve.wait_ge(x_landed[1], 16)
            dve.scalar_tensor_tensor(xs[:, 1, D // 2:D], xr[:, 1, D // 2:D], 1.0, xr[:, 1, D // 2:D], ALU.mult, ALU.mult,
                                     accum_out=sst[:, 0:1]).then_inc(ss_dve, 1)
            dve.wait_ge(ss_dve, 2)
            dve.wait_ge(ss_act, 2)
            dve.tensor_tensor(ss0[:, 1:2], ss0[:, 1:2], sst[:, 0:1], ALU.add).then_inc(ss_dve, 1)
            dve.wait_ge(r0_done, 2)
            for m, n in ((0, 0), (0, 1), (1, 1)):
                half = slice(n * D // 2, (n + 1) * D // 2)
                dve.tensor_scalar(xs[:, m, half], xr[:, m, half], r0[:, m:m + 1], None, ALU.mult).then_inc(xs_dve, 1)
            for kt in range(KT):
                dve.wait_ge(u_hi, kt + 1)
                dve.scalar_tensor_tensor(u[:, kt, 1, :], ps[:, 4 + kt % 4, 0:TOK], vec[:, V_PRE + kt:V_PRE + kt + 1],
                                         hi_view(u[:, kt, 0, :]), ALU.mult, ALU.subtract).then_inc(u_lo, 1)
                if kt % CK == CK - 1:
                    split(kt // CK)

            def masked(n):
                dve.wait_ge(z_made, n + 1)
                dve.tensor_tensor(zm[:, n % 2], ps[:, 5 + n % 2, 0:SM], mask, ALU.add).then_inc(zm_done, 1)

            def softplus(n):
                dve.wait_ge(lg_done, n + 1)
                dve.scalar_tensor_tensor(sp[:, n % 2], zm[:, n % 2], 0.0, lg, ALU.max, ALU.add).then_inc(sp_done, 1)

            def log_weights(n):
                dve.wait_ge(sum_made, n + 1)
                if n >= 4:
                    dve.wait_ge(o_made, n // 2 - 1)
                dve.scalar_tensor_tensor(wt[:, n % 4], ps[:, 5 + n % 2, 0:SM], 0.0, mask,
                                         ALU.min, ALU.add).then_inc(lw_done, 1)

            def head_pair_out(n):
                kt = n // 2
                dve.wait_ge(o_hi, kt + 1)
                dve.scalar_tensor_tensor(ffn[:, kt, 1, :], ps[:, 7, (kt % 2) * SEQ:(kt % 2 + 1) * SEQ],
                                         vec[:, V_MIX + kt:V_MIX + kt + 1], hi_view(ffn[:, kt, 0, :]),
                                         ALU.mult, ALU.subtract).then_inc(o_lo, 1)
                dve.wait_ge(o_sq, kt + 1)
                if kt == 0:
                    dve.tensor_copy(acc_o, sq_o).then_inc(o_acc, 1)
                else:
                    dve.wait_ge(o_acc, kt)
                    dve.tensor_tensor(acc_o, acc_o, sq_o, ALU.add).then_inc(o_acc, 1)

            def both(r):
                return r.rearrange("p (a t) -> p a t", a=1).to_broadcast([P, 2, SEQ])

            def add_squares(j):
                dve.wait_ge(y_sq, j + 1)
                if j == 0:
                    dve.tensor_copy(accy, sqy[:, 0]).then_inc(y_acc, 1)
                else:
                    dve.wait_ge(y_acc, j)
                    dve.tensor_tensor(accy, accy, sqy[:, j % 2], ALU.add).then_inc(y_acc, 1)

            def input_lo(j):
                for kt in (2 * j, 2 * j + 1):
                    dve.wait_ge(h2_hi, kt + 1)
                    dve.scalar_tensor_tensor(u[:, kt, 1, 0:SEQ], xT[:, kt, :], vec[:, V_FFN + kt:V_FFN + kt + 1],
                                             hi_view(u[:, kt, 0, 0:SEQ]), ALU.mult, ALU.subtract).then_inc(h2_lo, 1)

            for q in range(WSLOTS, Q_FFN + CK):
                if q < Q_FFN + CK - 1:
                    split(q)
                if q - 5 in HEAD_AT:
                    log_weights(HEAD_AT[q - 5])
                if q - 3 in HEAD_AT:
                    masked(HEAD_AT[q - 3])
                if q - 7 in HEAD_AT and HEAD_AT[q - 7] % 2:
                    head_pair_out(HEAD_AT[q - 7])
                for i in range(2):
                    if q - 4 == Q_CONV + 2 * i * CK + 2 * CK - 1:
                        dve.wait_ge(a_kept, i + 1)
                        dve.wait_ge(gate_sig, i + 1)
                        dve.tensor_tensor(glu[:, 2 * i:2 * i + 2, GP:GP + TOK], a_s, sg, ALU.mult).then_inc(glu_done, 1)
                w = q - Q_TAPS
                if 0 <= w < TAPS:
                    if w == 0:
                        dve.wait_ge(vec_done, 2)
                        dve.wait_ge(pads_ready, 1)
                        dve.wait_ge(glu_done, 2)
                    for t in range(VT):
                        src = glu[:, t, META + w:META + w + SEQ]
                        tap = dw[:, w * CT + t:w * CT + t + 1]
                        if w == 0:
                            dve.tensor_scalar(cy[:, t, :], src, tap, vec[:, V_BDW + t:V_BDW + t + 1],
                                              ALU.mult, ALU.add).then_inc(tap_done, 1)
                        else:
                            dve.wait_ge(tap_done, (w - 1) * VT + t + 1)
                            dve.scalar_tensor_tensor(cy[:, t, :], src, tap, cy[:, t, :],
                                                     ALU.mult, ALU.add).then_inc(tap_done, 1)
                if q - 3 in HEAD_AT:
                    softplus(HEAD_AT[q - 3])
                if q == Q_POOL + 2 * CK + LAG + 1:
                    dve.wait_ge(pu_kept, 2)
                    src = pu
                    for n in range(NPG):
                        d = 1 << n
                        lo = 2 * d - 1
                        dst = (pw0, pw1)[n % 2]
                        dve.tensor_tensor(dst[:, n:NPG, lo:TOK], src[:, n:NPG, lo:TOK], src[:, n:NPG, lo - d:TOK - d],
                                          ALU.add).then_inc(pool_step, 1)
                        dve.wait_ge(pool_step, 2 * n + 1)
                        dve.scalar_tensor_tensor(pooled[:, n, :], dst[:, n, META:TOK], 1.0 / (2 * d), pu[:, n, META:TOK],
                                                 ALU.mult, ALU.subtract).then_inc(pool_step, 1)
                        src = dst
                if q == PE_SSP + LAG:
                    dve.wait_ge(rp_done, 1)
                    for t in range(PT):
                        g = V_MIX + DA // P + t
                        dve.scalar_tensor_tensor(mf[:, t, :], mf[:, t, :], vec[:, g:g + 1], rside,
                                                 ALU.mult, ALU.mult).then_inc(pn_done, 1)
                if q == PE_SSP + LAG + 1:
                    dve.wait_ge(pool_hi, 1)
                    at = DA // P
                    dve.tensor_tensor(ffn[:, at:at + PT, 1, :], mf, hi_view(ffn[:, at:at + PT, 0, :]),
                                      ALU.subtract).then_inc(pool_lo, 1)
                if q == PE_LNM + LAG:
                    dve.wait_ge(lnm_made, 1)
                    for t in range(CT):
                        dve.scalar_tensor_tensor(cy[:, t, :], ps[:, 0, 0:SEQ], -1.0 / DC, cy[:, t, :],
                                                 ALU.mult, ALU.add).then_inc(ln_cent, 1)
                if q == PE_LNV + LAG + 1:
                    dve.wait_ge(ln_r, 1)
                    for t in range(CT):
                        dve.scalar_tensor_tensor(cy[:, t, :], cy[:, t, :], vec[:, V_LNG + t:V_LNG + t + 1], rside,
                                                 ALU.mult, ALU.mult).then_inc(ln_y, 1)
                if q == PE_SSC + LAG:
                    dve.wait_ge(rc_done, 1)
                    for t in range(CT):
                        g = V_MIX + (DA + DP) // P + t
                        dve.scalar_tensor_tensor(mf[:, t, :], cy[:, t, :], vec[:, g:g + 1], rside,
                                                 ALU.mult, ALU.mult).then_inc(cn_done, 1)
                if q == PE_SSC + LAG + 1:
                    dve.wait_ge(conv_hi, 1)
                    at = (DA + DP) // P
                    dve.tensor_tensor(ffn[:, at:KT, 1, :], mf, hi_view(ffn[:, at:KT, 0, :]),
                                      ALU.subtract).then_inc(conv_lo, 1)
                if q in T_AT:
                    j = T_AT[q]
                    dve.wait_ge(chunks_used, q - 3)
                    dve.wait_ge(ra_done, 1)
                    if j:
                        dve.wait_ge(y_done, j)
                    dve.tensor_tensor(tb, ps[:, attn_bank[j], :].rearrange("p (m t) -> p m t", m=2), both(ra),
                                      ALU.mult).then_inc(t_done, 1)
                if q == Q_FFN + CK - 2:
                    add_squares(NOB - 2)
                if q in Y_AT:
                    j = Y_AT[q]
                    if 0 < j < NOB - 1:
                        add_squares(j - 1)
                    dve.wait_ge(chunks_used, q - 3)
                    dve.wait_ge(t_done, j + 1)
                    dve.tensor_tensor(y[:, 2 * j:2 * j + 2, :], tb,
                                      ps[:, side_bank[j], :].rearrange("p (m t) -> p m t", m=2),
                                      ALU.add).then_inc(y_done, 1)

            split(Q_FFN + CK - 1)
            dve.wait_ge(r1_done, 1)
            for j in range(NOB + 1):
                if j < NOB:
                    dve.wait_ge(y_gain, 2 * j + 2)
                    if j >= 2:
                        dve.wait_ge(h2_done, j - 1)
                    dve.tensor_tensor(th[:, j % 2], y[:, 2 * j:2 * j + 2, :], both(r1), ALU.mult).then_inc(th_done, 1)
                if j == 0:
                    continue
                if j >= 2:
                    input_lo(j - 2)
                pair = slice(2 * j - 2, 2 * j)
                dve.wait_ge(th_done, j)
                dve.tensor_tensor(xT[:, pair, :], th[:, (j - 1) % 2], xT[:, pair, :], ALU.add).then_inc(h2_done, 1)
                if j in (6, 7):
                    split(Q_FFN + WSLOTS + j - 6)
            input_lo(NOB - 1)
            for q in range(Q_FFN + WSLOTS + 2, Q_FFN + 2 * CK + 2):
                split(q)

            def halves(ap):
                return ap.rearrange("p (a t) -> p a t", a=2)

            def gate_evac(i, end=Q_FFN + CK):
                dve.wait_ge(chunks_used, i * 2 * CK + end)
                dve.tensor_tensor(halves(tmp_ffn[:, 0, :]), halves(ps[:, 0, :]), both(r2), ALU.mult).then_inc(gs_done, 1)

            def up_evac(i):
                dve.wait_ge(chunks_used, i * 2 * CK + (Q_FFN + 2 * CK))
                dve.tensor_tensor(halves(tmp_ffn[:, 2, :]), halves(ps[:, 1, :]), both(r2), ALU.mult).then_inc(us_done, 1)
                dve.wait_ge(silu_done, i + 1)
                dve.wait_ge(us_done, i + 1)
                dve.tensor_tensor(tmp_ffn[:, 3, :], tmp_ffn[:, 1, :], tmp_ffn[:, 2, :], ALU.mult).then_inc(p_done, 1)
                sl, us, p = (tmp_ffn[:, n, :].rearrange("p (a t) -> p a t", a=2) for n in (1, 2, 3))
                dve.tensor_tensor(ffn[:, bass.ds(2 * i, 2), 0, :], sl, us, ALU.mult).then_inc(f_hi, 1)
                dve.wait_ge(f_hi, i + 1)
                dve.wait_ge(p_done, i + 1)
                dve.tensor_tensor(ffn[:, bass.ds(2 * i, 2), 1, :], p, hi_view(ffn[:, bass.ds(2 * i, 2), 0, :]),
                                  ALU.subtract).then_inc(f_lo, 1)

            dve.wait_ge(r2_done, 1)
            dve.wait_ge(rows_made, 2 * DN)
            gate_evac(0, Q_FFN + 2 * CK - 1)
            split(Q_FFN + 2 * CK + 2)
            up_evac(0)
            for s in range(3, 2 * CK):
                split(Q_FFN + 2 * CK + s)
            with dve.Fori(1, NFB - 1) as i:
                gate_evac(i)
                for s in range(CK):
                    split_lo(i * 2 * CK + (Q_FFN + 2 * CK + s), s)
                up_evac(i)
                for s in range(CK):
                    split_lo(i * 2 * CK + (Q_FFN + 3 * CK + s), s)
            gate_evac(NFB - 1)
            for q in range(Q_DOWN, Q_DOWN + DN * DCH + 4):
                if q < Q_DOWN + DN * DCH:
                    split(q)
                if q == Q_DOWN + 3:
                    up_evac(NFB - 1)
                n, rest = (q - 4 - Q_DOWN) // DCH, (q - 4 - Q_DOWN) % DCH
                if q - 4 >= Q_DOWN and rest == DCH - 1:
                    cols = slice(n * DCOLS, (n + 1) * DCOLS)
                    dve.wait_ge(chunks_used, q - 3)
                    if n == 0:
                        dve.wait_ge(gbc_landed, 16)
                    for m in reversed(range(NQ)):
                        if m == 0:
                            dve.wait_ge(dsq_done, NQ * n + 1)
                        dve.tensor_tensor(f_acc[:, m, cols], ps[:, 2 + 2 * (n % 2) + m, :], gbc[:, cols],
                                          ALU.mult).then_inc(f_done, 1)
                    dve.wait_ge(f_done, NQ * (n + 1))
                    dve.sem_inc(down_free, 1)
            dve.wait_ge(dsq_done, NQ * DN)
            dve.tensor_reduce(sst, ssd, AX.X, ALU.add).then_inc(sst_done, 1)
            dve.wait_ge(rd_done, 1)
            for m, cols in OUT_PIECES:
                dve.scalar_tensor_tensor(f_acc[:, m, cols], f_acc[:, m, cols], rd[:, m:m + 1],
                                         h2rows[:, m, cols], ALU.mult, ALU.add).then_inc(res_done, 1)

        @block.tensor
        def _(pe):
            def products(q, slot, kts, rhs, outs, first, last, one_bank):
                pe.wait_ge(lo_done, q + 1)
                for k, kt in enumerate(kts):
                    x_hi, x_lo = rhs(kt)
                    for m in range(2):
                        at = slice(k * BLK + m * P, k * BLK + (m + 1) * P)
                        start = first and k == 0
                        pe.matmul(outs[m], w_hi[:, slot, at], x_hi, start=start and not (one_bank and m), stop=False,
                                  skip_group_check=True)
                        pe.matmul(outs[m], w_hi[:, slot, at], x_lo, start=False, stop=False, skip_group_check=True)
                        mm = pe.matmul(outs[m], w_lo[:, slot, at], x_hi, start=False,
                                       stop=last and k == len(kts) - 1, skip_group_check=True)
                mm.then_inc(chunks_used, 1)

            def normed(kt, lo=0):
                return u[:, kt, 0, lo:TOK], u[:, kt, 1, lo:TOK]

            def ffn_input(kt):
                return u[:, kt, 0, 0:SEQ], u[:, kt, 1, 0:SEQ]

            def merged(kt):
                return ffn[:, kt, 0, :], ffn[:, kt, 1, :]

            def two(bank):
                return [ps[:, bank, 0:SEQ], ps[:, bank, SEQ:2 * SEQ]]

            def wide(bank):
                return [ps[:, bank, 0:TOK], ps[:, bank + 1, 0:TOK]]

            def column_sums(dst, srcs, made):
                for n, s in enumerate(srcs):
                    mm = pe.matmul(dst, ones, s, start=n == 0, stop=n == len(srcs) - 1)
                mm.then_inc(made, 1)

            def keep_warm(n):
                for _ in range(n):
                    pe.matmul(ps[:, 1, 0:P], ones, ones, start=True, stop=True)

            pe.wait_ge(const_step, 2)
            keep_warm(WARM_LOAD)
            pe.wait_ge(const_ready, 1)
            pe.wait_ge(grow_landed, 16)
            pe.transpose(ps[:, 0, 0:KT], grow[0:KT, :], ident[0:KT, 0:KT]).then_inc(grow_turned, 1)
            keep_warm(WARM_ROWS)

            def turn_rows(kts):
                for kt in kts:
                    if kt in (0, KT // 2):
                        pe.wait_ge(xs_dve, 1 if kt == 0 else 3)
                    if kt == 0:
                        pe.wait_ge(xs_act, 2)
                    if kt >= 4:
                        pe.wait_ge(u_lo, kt - 3)
                    b, cols = 4 + kt % 4, slice(kt * P, (kt + 1) * P)
                    pe.transpose(ps[:, b, 0:META], xsm[0:META, cols], ident[0:META, 0:META])
                    pe.transpose(ps[:, b, META:META + P], xs[:, 0, cols], ident)
                    pe.transpose(ps[:, b, META + P:TOK], xs[:, 1, cols], ident).then_inc(u_made, 1)

            turn_rows(range(0, CK))
            keep_warm(WARM_PARTS)

            def early_work(q):
                if q < CK - 1:
                    turn_rows(range((q + 1) * CK, (q + 2) * CK))
                    if q == 0:
                        keep_warm(WARM_PARTS)
                if q == VEC_AT:
                    pe.wait_ge(u_lo, KT)
                    pe.wait_ge(vec_landed, 16 * 8)
                    pe.transpose(ps[:, 7, 0:NB], vrow[0:NB, :], ident[0:NB, 0:NB])
                    pe.transpose(ps[:, 7, P:P + TAPS * CT], drow[0:TAPS * CT, :],
                                 ident[0:TAPS * CT, 0:TAPS * CT]).then_inc(vec_turned, 1)
                if 0 <= q - TURN_AT < NOB:
                    j = q - TURN_AT
                    if j == 3:
                        pe.wait_ge(vec_done, 2)
                    if j >= 4:
                        pe.wait_ge(xt_kept, j - 3)
                    for kt in (2 * j, 2 * j + 1):
                        for m in range(NQ):
                            at = (kt % 2 * NQ + m) * P
                            mm = pe.transpose(ps[:, 4 + j % 4, at:at + P], xr[:, m, kt * P:(kt + 1) * P], ident)
                    mm.then_inc(xt_made, 1)

            def proj(q0, outs, one_bank=False, lo=0):
                for s in range(CK):
                    early_work(q0 + s)
                    pe.wait_ge(u_lo, (s + 1) * CK)
                    products(q0 + s, s, range(s * CK, (s + 1) * CK), lambda kt: normed(kt, lo), outs,
                             s == 0, s == CK - 1, one_bank)

            for i in range(2):
                if i:
                    pe.wait_ge(a_kept, i)
                proj(i * 2 * CK + Q_CONV, wide(0))
                if i:
                    pe.wait_ge(gate_sig, i)
                proj(i * 2 * CK + (Q_CONV + CK), wide(2))
            pe.wait_ge(a_kept, 2)
            proj(Q_POOL, wide(0))
            pe.wait_ge(xt_kept, NOB)
            proj(Q_POOL + CK, wide(pool_bank[1]))

            tiles_of = ((S0, META), (S1, P), (S2, 2 * P))

            def scores(n):
                g, t, half = n // HPG, n % HPG // 2, slice(n % 2 * DH, n % 2 * DH + DH)
                z = ps[:, 5 + n % 2, :]
                pe.wait_ge(k_kept, g + 1)
                pe.wait_ge(q_kept, g + 1)
                if g == 0:
                    pe.wait_ge(pads0, 2)
                if n >= 2:
                    pe.wait_ge(lw_done, n - 1)
                pe.wait_ge(vt_kept, 2 * (g + 1))
                for k, (at, t0) in enumerate(tiles_of):
                    mm = pe.matmul(z[:, at:at + TOK - t0], kb[g % 2][half, t, k * P:(k + 1) * P],
                                   qb[g % 2][half, t, t0 - META:SEQ], start=k == 0, stop=k == 2, skip_group_check=True)
                mm.then_inc(z_made, 1)

            def later_sums(n):
                z, s = ps[:, 5 + n % 2, :], sp[:, n % 2]
                pe.wait_ge(sp_done, n + 1)
                if n == 0:
                    pe.wait_ge(const_ready, 2)
                pe.matmul(z[:, 0:SM], negtri, s[:, 0:SM], start=False, stop=False, skip_group_check=True)
                pe.matmul(z[:, P - META:SEQ], negones, s[:, S1:S2], start=False, stop=False, skip_group_check=True)
                n2 = SM - S2
                step = S2 - SEQ
                ends = z[:, SEQ - step:SEQ + step].rearrange("p (a t) -> p a t", a=2)[:, :, step - n2:step]
                pe.matmul(ends, negones, s[:, S2:SM].rearrange("p (a t) -> p a t", a=1).to_broadcast([P, 2, n2]),
                          start=False, stop=True, skip_group_check=True).then_inc(sum_made, 1)

            def values(kt):
                g, t = 2 * kt // HPG, 2 * kt % HPG // 2
                pe.wait_ge(wt_done, 2 * kt + 2)
                if kt:
                    pe.wait_ge(o_lo, kt)
                for k, (at, t0) in enumerate(tiles_of):
                    for e in range(2):
                        mm = pe.matmul(ps[e * DH:(e + 1) * DH, 7, t * SEQ + t0 - META:(t + 1) * SEQ],
                                       vT[g % 2][:, k, t * P + e * DH:t * P + (e + 1) * DH],
                                       wt[:, (2 * kt + e) % 4, at:at + TOK - t0], start=k == 0, stop=k == 2,
                                       skip_group_check=True)
                mm.then_inc(o_made, 1)

            def side_work(q):
                if q - 4 in HEAD_AT and HEAD_AT[q - 4] % 2:
                    values(HEAD_AT[q - 4] // 2)
                if q - 2 in HEAD_AT:
                    later_sums(HEAD_AT[q - 2])
                if q in HEAD_AT:
                    scores(HEAD_AT[q])
                if q in VT_AT:
                    g = VT_AT[q]
                    pe.wait_ge(v_kept, g + 1)
                    if g == 0:
                        pe.wait_ge(pm_done, NPG + 1)
                        pe.wait_ge(pads0, 2)
                    else:
                        pe.wait_ge(lw_done, HPG * g)
                    for m in range(2):
                        for k in range(3):
                            mm = pe.transpose(ps[:, 5 + m, k * P:(k + 1) * P], vb[g % 2][:, m, k * P:(k + 1) * P], ident)
                    mm.then_inc(vt_made, 1)
                if q == PE_MIX:
                    pe.wait_ge(sw_landed, 32)
                    pe.wait_ge(pu_kept, 2)
                    pe.wait_ge(pool_step, 2 * NPG)
                    for g in range(NPG):
                        mm = pe.matmul(ps[:, 5 + g // 2, (g % 2) * SEQ:(g % 2 + 1) * SEQ], wpl[:, g, :],
                                       pooled[:, g, :], start=True, stop=True)
                    mm.then_inc(mix_made, 1)
                if q == PE_SSP:
                    pe.wait_ge(tiles_added, 2)
                    column_sums(ps[:, 7, 0:SEQ], [sq4[:, 0, :]], ssp_made)
                if q == PE_LNM:
                    pe.wait_ge(tiles_added, 4)
                    pe.wait_ge(k_kept, (q - SC) // PER_G + 1)
                    column_sums(ps[:, 0, 0:SEQ], [sq4[:, 0, :]], lnm_made)
                if q == PE_LNV:
                    pe.wait_ge(tiles_added, 6)
                    column_sums(ps[:, 0, 0:SEQ], [sq4[:, 0, :]], lnv_made)
                if q in (PE_PW, PE_PW + 1):
                    b = q - PE_PW
                    pe.wait_ge(ln_act, CT)
                    pe.wait_ge(k_kept, (PE_PW - SC) // PER_G + 1)
                    for m in range(2):
                        d0 = (2 * b + m) * P
                        for t in range(CT):
                            mm = pe.matmul(ps[:, b, m * SEQ:(m + 1) * SEQ], wpw[:, t, d0:d0 + P], mf[:, t, :],
                                           start=t == 0, stop=t == CT - 1)
                    mm.then_inc(pw_made, 1)
                if q == PE_SSC:
                    pe.wait_ge(tiles_added, 8)
                    pe.wait_ge(v_kept, GROUPS)
                    column_sums(ps[:, 2, 0:SEQ], [sq4[:, 0, :]], ssc_made)
                if q == PE_SSA:
                    pe.wait_ge(o_acc, DA // P)
                    pe.wait_ge(o_lo, DA // P)
                    column_sums(ps[:, 7, 0:SEQ], [acc_o], ssa_made)

            for g in range(GROUPS):
                for b, outs in enumerate((wide(2), two(4), wide(0))):
                    q0 = Q_ATT + g * PER_G + b * CK
                    if b == 0:
                        pe.wait_ge(gate_sig, 2)
                        if g:
                            pe.wait_ge(v_kept, g)
                    if b == 1:
                        pe.wait_ge(xt_kept, NOB)
                        if g:
                            pe.wait_ge(q_kept, g)
                    if b == 2:
                        pe.wait_ge(pu_kept, 1)
                        if g:
                            pe.wait_ge(k_kept, g)
                    if b == 2 and q0 > PE_PW:
                        pe.wait_ge(oc_done, 2)
                    if b == 2 and PE_LNV < q0 < PE_PW:
                        pe.wait_ge(ln_r, 1)
                    for s in range(CK):
                        side_work(q0 + s)
                        lo = META if b == 1 else 0
                        products(q0 + s, s, range(s * CK, (s + 1) * CK), lambda kt: normed(kt, lo), outs,
                                 s == 0, s == CK - 1, b == 1)

            y_of = {}
            for n, (part, j) in enumerate(out_parts):
                bank = (side_bank if part == "side" else attn_bank)[j]
                kt0 = DA // P if part == "side" else 0
                for s in range(OC):
                    q = Q_OUT + n * OC + s
                    side_work(q)
                    if s == 0:
                        if bank in y_of:
                            pe.wait_ge(y_done, y_of[bank] + 1)
                        elif part == "side":
                            pe.wait_ge((k_kept, k_kept, rc_done, v_kept, q_kept)[bank],
                                       (GROUPS, GROUPS, 1, GROUPS, GROUPS)[bank])
                        elif bank == 7:
                            pe.wait_ge(ra_done, 1)
                        else:
                            pe.wait_ge(lw_done, NH)
                        y_of[bank] = j
                    if part == "side":
                        pe.wait_ge(pool_lo, 1)
                        if s:
                            pe.wait_ge(conv_lo, 1)
                    else:
                        pe.wait_ge(o_lo, (s + 1) * CK)
                    products(q, q % WSLOTS, range(kt0 + s * CK, kt0 + (s + 1) * CK), merged, two(bank),
                             s == 0, s == OC - 1, True)

            pe.wait_ge(y_acc, NOB - 1)
            for h in range(2):
                pe.matmul(ps[:, 2, 0:SEQ], ones, accy[:, h, :], start=h == 0, stop=False)
            pe.wait_ge(y_sq, NOB)
            for h in range(2):
                mm = pe.matmul(ps[:, 2, 0:SEQ], ones, sqy[:, (NOB - 1) % 2, h, :], start=False, stop=h == 1)
            mm.then_inc(ssy_made, 1)
            for _ in range(WARM_FFN):
                pe.matmul(ps[:, 4, 0:SEQ], ffn[:, 0, 0, 0:P], ffn[:, 0, 0, :], start=True, stop=True)

            def fresh_input(kt):
                pe.wait_ge(h2_lo, kt + 1)
                return ffn_input(kt)

            for s in range(CK):
                if s == CK - 1:
                    pe.wait_ge(h2_acc, NOB - 1)
                    column_sums(ps[:, 7, 0:SEQ], [accy[:, 0, :], accy[:, 1, :]], ss2_made)
                for b in range(2):
                    q = Q_FFN + 2 * s + b
                    products(q, q % WSLOTS, range(s * CK, (s + 1) * CK), ffn_input if b else fresh_input, two(b),
                             s == 0, s == CK - 1, True)
                    for m in range(0 if b else NQ):
                        n = NQ * s + m
                        if n >= 4:
                            pe.wait_ge(rows_kept, n - 3)
                        for k in range(4):
                            mm = pe.transpose(ps[:, 3 + n % 4, k * P:(k + 1) * P],
                                              xT[:, s * 4 + k, m * P:(m + 1) * P], ident)
                        mm.then_inc(rows_made, 1)

            def ffn_block(q0, bank):
                for s in range(CK):
                    products(q0 + s, s, range(s * CK, (s + 1) * CK), ffn_input, two(bank), s == 0, s == CK - 1, True)

            with pe.Fori(1, NFB) as i:
                pe.wait_ge(gs_done, i)
                ffn_block(i * 2 * CK + Q_FFN, 0)
                pe.wait_ge(us_done, i)
                ffn_block(i * 2 * CK + (Q_FFN + CK), 1)

            with pe.Fori(0, DN // 2) as i:
                for b in range(2):
                    pe.wait_ge(down_free, i * 4 + (2 * b + 2))
                    for d in range(DCH):
                        slot = (b * DCH + d) % WSLOTS
                        pe.wait_ge(lo_done, i * 2 * DCH + (Q_DOWN + b * DCH + d + 1))
                        pe.wait_ge(f_lo, d + 1)
                        for k in range(2):
                            kt = 2 * d + k
                            mv = slice(k * DCOLS, (k + 1) * DCOLS)
                            for m in range(NQ):
                                o = ps[:, 2 + 2 * b + m, :]
                                rows_m = slice(m * P, (m + 1) * P)
                                first, last = d == 0 and k == 0, d == DCH - 1 and k == 1
                                pe.matmul(o, ffn[:, kt, 0, rows_m], w_hi[:, slot, mv], start=first, stop=False)
                                pe.matmul(o, ffn[:, kt, 0, rows_m], w_lo[:, slot, mv], start=False, stop=False)
                                mm = pe.matmul(o, ffn[:, kt, 1, rows_m], w_hi[:, slot, mv], start=False, stop=last)
                        mm.then_inc(chunks_used, 1)


_INS = ['x', 'meta_tokens', 'pre_mix_g', 'w_in', 'w_pool', 'pool_scale', 'w_dw', 'b_dw', 'conv_ln_g', 'conv_ln_b',
        'w_pw', 'mix_out_g', 'w_out', 'post_mix_g', 'pre_ffn_g', 'w_gate', 'w_up', 'w_down', 'post_ffn_g']


def kernel(**inputs):
    import numpy as np
    import concourse.bacc as bacc
    from concourse.bass_utils import run_bass_kernel_spmd

    nc = bacc.Bacc("TRN2", target_bir_lowering=False, num_devices=1)
    arrays, args = {}, []
    for name in _INS:
        a = np.ascontiguousarray(inputs[name])
        arrays[f"in_{name}"] = a
        args.append(nc.dram_tensor(f"in_{name}", a.shape, mybir.dt.from_np(a.dtype), kind="ExternalInput").ap())
    out = nc.dram_tensor("out", inputs["x"].shape, F32, kind="ExternalOutput").ap()
    build_trunk(nc, *args, out)
    r = run_bass_kernel_spmd(nc, [arrays], core_ids=[0])
    return r.results[0]["out"]
```
